# Optimizing a Trainium2 kernel written in Bass

```python
import jax
import jax.numpy as jnp
from jax import lax
import numpy as np

D_MODEL = 1024
BATCH = 1
SEQ = 1024
DEPTH = 1
DEC_BATCH = 8
DEC_SEQ = 1
PAST_LEN = 1024
PAGE_SIZE = 128

N_META = 16
BLOCK = 128
FOX_HEADS = 8
FOX_DH = 64
FOX_W = FOX_HEADS * FOX_DH
GLA_HEADS = 4
GLA_DK = 64
GLA_DV = 128
GLA_K = GLA_HEADS * GLA_DK
GLA_V = GLA_HEADS * GLA_DV
GLA_RANK = 16
GLA_TAU = 16.0
D_FF = ((-(-8 * D_MODEL // 3) + 255) // 256) * 256
LN_EPS = 1e-5
NORM_EPS = 1e-6
NEG_INF = -1e30
ALPHA = (2.0 * DEPTH) ** 0.25
BETA = (8.0 * DEPTH) ** -0.25
IN_SPLITS = (FOX_W, FOX_W, FOX_W, FOX_HEADS, GLA_K, GLA_K, GLA_V, GLA_V, GLA_RANK, D_MODEL, D_MODEL)
N_IN = sum(IN_SPLITS)

kernel_name = 'fox_gla_hybrid_step'

def _layer_norm(x, g, b):
    xf = x.astype(jnp.float32)
    mu = jnp.mean(xf, axis=-1, keepdims=True)
    var = jnp.mean(jnp.square(xf - mu), axis=-1, keepdims=True)
    y = (xf - mu) * lax.rsqrt(var + LN_EPS) * g.astype(jnp.float32) + b.astype(jnp.float32)
    return y.astype(x.dtype)

def _project_in(x, w_in, b_f, w_a2, b_a):
    lead = x.shape[:-1]
    idx = np.cumsum(IN_SPLITS)[:-1].tolist()
    qa, ka, va, fa, qb, kb, vb, rb, alr, ga, gb = jnp.split(x @ w_in, idx, axis=-1)
    heads = lambda t, h: t.reshape(*lead, h, t.shape[-1] // h)
    lf = jax.nn.log_sigmoid((fa + b_f).astype(jnp.float32))
    lg = jax.nn.log_sigmoid((alr @ w_a2 + b_a).astype(jnp.float32)) / GLA_TAU
    return (heads(qa, FOX_HEADS), heads(ka, FOX_HEADS), heads(va, FOX_HEADS), lf,
            heads(qb, GLA_HEADS) * (GLA_DK ** -0.5), heads(kb, GLA_HEADS), heads(vb, GLA_HEADS),
            heads(lg, GLA_HEADS), rb, ga, gb)

def _fox_prompt(q, k, v, lf):
    b, l, h, dh = q.shape
    pad = (-l) % BLOCK
    lp = l + pad
    nb = lp // BLOCK
    pw = ((0, 0), (pad, 0), (0, 0), (0, 0))
    q, k, v = jnp.pad(q, pw), jnp.pad(k, pw), jnp.pad(v, pw)
    c = jnp.cumsum(jnp.pad(lf, pw[:3]), axis=1)
    c_keys = c.transpose(0, 2, 1)
    pos = jnp.arange(lp)
    q_blocks = q.reshape(b, nb, BLOCK, h, dh).transpose(1, 0, 2, 3, 4)
    c_blocks = c.reshape(b, nb, BLOCK, h).transpose(1, 0, 3, 2)
    p_blocks = pos.reshape(nb, BLOCK)
    scale = dh ** -0.5

    def block(args):
        qi, ci, pi = args
        s = jnp.einsum('bqhd,bkhd->bhqk', qi, k).astype(jnp.float32) * scale
        s = s + ci[..., None] - c_keys[:, :, None, :]
        mask = (pos[None, :] <= pi[:, None]) & (pos[None, :] >= pad)
        s = jnp.where(mask, s, NEG_INF)
        p = jax.nn.softmax(s, axis=-1).astype(v.dtype)
        return jnp.einsum('bhqk,bkhd->bqhd', p, v)

    o = lax.map(block, (q_blocks, c_blocks, p_blocks))
    return o.transpose(1, 0, 2, 3, 4).reshape(b, lp, h, dh)[:, pad:]

def _fox_sample(q, k, v, lf, ck, cv, clf, page_table):
    b, t, h, dh = q.shape
    k_all = jnp.concatenate([ck[page_table].reshape(b, -1, h, dh), k.astype(ck.dtype)], axis=1)
    v_all = jnp.concatenate([cv[page_table].reshape(b, -1, h, dh), v.astype(cv.dtype)], axis=1)
    lf_all = jnp.concatenate([clf[page_table].reshape(b, -1, h).astype(jnp.float32), lf], axis=1)
    past = k_all.shape[1] - t
    c = jnp.cumsum(lf_all, axis=1).transpose(0, 2, 1)
    s = jnp.einsum('bqhd,bkhd->bhqk', q, k_all.astype(q.dtype)).astype(jnp.float32) * dh ** -0.5
    s = s + c[:, :, past:, None] - c[:, :, None, :]
    kpos = jnp.arange(past + t)
    qpos = past + jnp.arange(t)
    s = jnp.where(kpos[None, :] <= qpos[:, None], s, NEG_INF)
    p = jax.nn.softmax(s, axis=-1).astype(v_all.dtype)
    return jnp.einsum('bhqk,bkhd->bqhd', p, v_all)

def _gla_prompt(q, k, v, lg):
    b, l, h, dk = q.shape
    dv = v.shape[-1]
    pad = (-l) % BLOCK
    lp = l + pad
    nc = lp // BLOCK
    pw = ((0, 0), (pad, 0), (0, 0), (0, 0))

    def chunks(t):
        t = jnp.pad(t.astype(jnp.float32), pw)
        return t.reshape(b, nc, BLOCK, h, t.shape[-1]).transpose(1, 0, 3, 2, 4)

    causal = jnp.tril(jnp.ones((BLOCK, BLOCK), dtype=bool))

    def step(state, inp):
        qc, kc, vc, gc = inp
        bc = jnp.cumsum(gc, axis=2)
        diff = bc[:, :, :, None, :] - bc[:, :, None, :, :]
        decay = jnp.exp(jnp.where(causal[:, :, None], diff, -jnp.inf))
        scores = jnp.einsum('bhtsd,bhsd->bhts', qc[:, :, :, None, :] * decay, kc)
        o = (jnp.einsum('bhts,bhsv->bhtv', scores, vc)
             + jnp.einsum('bhtd,bhdv->bhtv', qc * jnp.exp(bc), state))
        b_last = bc[:, :, -1:, :]
        k_dec = kc * jnp.exp(b_last - bc)
        state = (jnp.exp(b_last[:, :, 0, :])[..., None] * state
                 + jnp.einsum('bhsd,bhsv->bhdv', k_dec, vc))
        return state, o

    s0 = jnp.zeros((b, h, dk, dv), jnp.float32)
    s_fin, o = lax.scan(step, s0, (chunks(q), chunks(k), chunks(v), chunks(lg)))
    o = o.transpose(1, 0, 3, 2, 4).reshape(b, lp, h, dv)[:, pad:]
    return o, s_fin

def _gla_sample(q, k, v, lg, state):
    def step(s, inp):
        qt, kt, vt, gt = inp
        s = jnp.exp(gt)[..., None] * s + kt[..., :, None] * vt[..., None, :]
        return s, jnp.einsum('bhd,bhdv->bhv', qt, s)

    tmaj = lambda t: t.astype(jnp.float32).transpose(1, 0, 2, 3)
    s_new, o = lax.scan(step, state.astype(jnp.float32), (tmaj(q), tmaj(k), tmaj(v), tmaj(lg)))
    return o.transpose(1, 0, 2, 3), s_new

def _merge(x, o_a, o_b, rb, ga, gb, gla_norm_g, w_pa, w_pb, w_o, g, b):
    lead = x.shape[:-1]
    ob = o_b.astype(jnp.float32)
    ob = ob * lax.rsqrt(jnp.mean(jnp.square(ob), axis=-1, keepdims=True) + NORM_EPS) * gla_norm_g.astype(jnp.float32)
    ob = (ob.reshape(*lead, GLA_V) * jax.nn.silu(rb.astype(jnp.float32))).astype(x.dtype)
    y_a = o_a.reshape(*lead, FOX_W).astype(x.dtype) @ w_pa
    y_b = ob @ w_pb
    mixed = jax.nn.sigmoid(ga) * y_a + jax.nn.sigmoid(gb) * y_b
    return _layer_norm(ALPHA * x + mixed @ w_o, g, b)

def _ffn(x, w_gate, w_up, w_down, g, b):
    hdn = jax.nn.silu(x @ w_gate) * (x @ w_up)
    return _layer_norm(ALPHA * x + hdn @ w_down, g, b)

def setup_inputs(seed: int = 0) -> dict:
    key = jax.random.key(seed)
    ks = jax.random.split(key, 24)
    n_pages = PAST_LEN // PAGE_SIZE
    n_used = DEC_BATCH * n_pages
    n_pool = n_used + max(1, n_used // 4)
    nrm = lambda k, shape, s: jax.random.normal(k, shape, jnp.float32) * s
    page_table = jax.random.permutation(ks[5], n_pool)[:n_used].reshape(DEC_BATCH, n_pages).astype(jnp.int32)
    return {
        'x_prompt': nrm(ks[0], (BATCH, SEQ, D_MODEL), 1.0),
        'x_sample': nrm(ks[1], (DEC_BATCH, DEC_SEQ, D_MODEL), 1.0),
        'cache_k': nrm(ks[2], (DEPTH, n_pool, PAGE_SIZE, FOX_HEADS, FOX_DH), 1.0),
        'cache_v': nrm(ks[3], (DEPTH, n_pool, PAGE_SIZE, FOX_HEADS, FOX_DH), 1.0),
        'cache_lf': jax.nn.log_sigmoid(nrm(ks[4], (DEPTH, n_pool, PAGE_SIZE, FOX_HEADS), 1.0)),
        'state_gla': nrm(ks[6], (DEPTH, DEC_BATCH, GLA_HEADS, GLA_DK, GLA_DV), 1.0),
        'page_table': page_table,
        'meta': nrm(ks[7], (N_META, D_MODEL), 1.0),
        'w_in': nrm(ks[8], (DEPTH, D_MODEL, N_IN), D_MODEL ** -0.5),
        'b_f': nrm(ks[9], (DEPTH, FOX_HEADS), 0.1),
        'w_a2': nrm(ks[10], (DEPTH, GLA_RANK, GLA_K), GLA_RANK ** -0.5),
        'b_a': nrm(ks[11], (DEPTH, GLA_K), 0.1),
        'gla_norm_g': 1.0 + nrm(ks[12], (DEPTH, GLA_DV), 0.1),
        'w_pa': nrm(ks[13], (DEPTH, FOX_W, D_MODEL), FOX_W ** -0.5),
        'w_pb': nrm(ks[14], (DEPTH, GLA_V, D_MODEL), GLA_V ** -0.5),
        'w_o': nrm(ks[15], (DEPTH, D_MODEL, D_MODEL), D_MODEL ** -0.5 * BETA),
        'ln1_g': 1.0 + nrm(ks[16], (DEPTH, D_MODEL), 0.1),
        'ln1_b': nrm(ks[17], (DEPTH, D_MODEL), 0.05),
        'w_gate': nrm(ks[18], (DEPTH, D_MODEL, D_FF), D_MODEL ** -0.5),
        'w_up': nrm(ks[19], (DEPTH, D_MODEL, D_FF), D_MODEL ** -0.5),
        'w_down': nrm(ks[20], (DEPTH, D_FF, D_MODEL), D_FF ** -0.5 * BETA),
        'ln2_g': 1.0 + nrm(ks[21], (DEPTH, D_MODEL), 0.1),
        'ln2_b': nrm(ks[22], (DEPTH, D_MODEL), 0.05),
    }

def reference(x_prompt, x_sample, cache_k, cache_v, cache_lf, state_gla, page_table,
              meta, w_in, b_f, w_a2, b_a, gla_norm_g, w_pa, w_pb, w_o, ln1_g, ln1_b,
              w_gate, w_up, w_down, ln2_g, ln2_b):
    bsz = x_prompt.shape[0]
    meta_b = jnp.broadcast_to(meta[None].astype(x_prompt.dtype), (bsz, N_META, D_MODEL))
    hp = jnp.concatenate([meta_b, x_prompt], axis=1)
    hs = x_sample
    kp_rows, vp_rows, lfp_rows, gp_states = [], [], [], []
    ks_rows, vs_rows, lfs_rows, gs_states = [], [], [], []
    for l in range(DEPTH):
        qa, ka, va, lf, qb, kb, vb, lg, rb, ga, gb = _project_in(hp, w_in[l], b_f[l], w_a2[l], b_a[l])
        o_a = _fox_prompt(qa, ka, va, lf)
        o_b, s_fin = _gla_prompt(qb, kb, vb, lg)
        hp = _merge(hp, o_a, o_b, rb, ga, gb, gla_norm_g[l], w_pa[l], w_pb[l], w_o[l], ln1_g[l], ln1_b[l])
        hp = _ffn(hp, w_gate[l], w_up[l], w_down[l], ln2_g[l], ln2_b[l])
        kp_rows.append(ka)
        vp_rows.append(va)
        lfp_rows.append(lf)
        gp_states.append(s_fin)
        qa, ka, va, lf, qb, kb, vb, lg, rb, ga, gb = _project_in(hs, w_in[l], b_f[l], w_a2[l], b_a[l])
        o_a = _fox_sample(qa, ka, va, lf, cache_k[l], cache_v[l], cache_lf[l], page_table)
        o_b, s_new = _gla_sample(qb, kb, vb, lg, state_gla[l])
        hs = _merge(hs, o_a, o_b, rb, ga, gb, gla_norm_g[l], w_pa[l], w_pb[l], w_o[l], ln1_g[l], ln1_b[l])
        hs = _ffn(hs, w_gate[l], w_up[l], w_down[l], ln2_g[l], ln2_b[l])
        ks_rows.append(ka)
        vs_rows.append(va)
        lfs_rows.append(lf)
        gs_states.append(s_new)
    y_prompt = hp[:, N_META:]
    y_sample = hs
    return (y_prompt, y_sample,
            jnp.stack(kp_rows), jnp.stack(vp_rows), jnp.stack(lfp_rows), jnp.stack(gp_states),
            jnp.stack(ks_rows), jnp.stack(vs_rows), jnp.stack(lfs_rows), jnp.stack(gs_states))


_drawn_inputs = setup_inputs


def setup_inputs(seed=0):
    import zlib

    import numpy as np

    out = dict(_drawn_inputs(seed))
    spreads = {}
    factors = {'gla_norm_g': 3.72}
    for name, (base, spread) in spreads.items():
        noise = np.random.default_rng([zlib.crc32(name.encode()), seed]).standard_normal(out[name].shape)
        drawn = base * np.exp(spread * noise) if base else spread * noise
        out[name] = jnp.asarray(drawn.astype(out[name].dtype))
    for name, factor in factors.items():
        out[name] = (out[name] * factor).astype(out[name].dtype)
    return out
```

```python
from contextlib import ExitStack

import numpy as np
import concourse.bass as bass
from concourse import mybir

F32 = mybir.dt.float32
F32R = mybir.dt.float32r
BF16 = mybir.dt.bfloat16
I32 = mybir.dt.int32
ALU = mybir.AluOpType
ACT = mybir.ActivationFunctionType
AX = mybir.AxisListType.X

P = 128
D = 1024
KT = D // P
META, SEQ, NB = 16, 1024, 8
TP = META + SEQ
T = TP + NB
NT = 9
TAIL = TP - 8 * P
CHUNKS = [(0, 352), (352, 352), (704, 344)]
FH, DH = 8, 64
FW = FH * DH
GH, GDK, GDV = 4, 64, 128
GK, GV = GH * GDK, GH * GDV
RANK = 16
TAU = 16.0
DFF = 2816
PAGE, NPAGE = 128, 8
NPOOL = 80
ALPHA = 2.0 ** 0.25
NEG = -1e30
O_FA = 3 * FW
O_QB = O_FA + FH
O_KB = O_QB + GK
O_VB = O_KB + GK
O_RB = O_VB + GV
O_AL = O_RB + GV
O_GA = O_AL + RANK
O_GB = O_GA + D

RING = 3
PAN_QKV = 1
PAN_GLA = PAN_QKV + 12
PAN_MERGE = PAN_GLA + 12
PAN_O = PAN_MERGE + 24
PAN_FFN = PAN_O + 8
FGROUPS = DFF // (2 * P)
PANELS = PAN_FFN + 6 * FGROUPS
ROW_ALR = 32


def width(t):
    return P if t < 8 else TAIL


SEG = 384
SEGS = -(-TP // SEG)
NI = 2 * NT
PER_SEG = SEG // P
GROUPS = 2 * SEGS


def probability_tiles():
    out = []
    for k in range(GROUPS):
        h, s = divmod(k, SEGS)
        q0, q1 = SEG * s, min(SEG * (s + 1), TP)
        n = -(-q1 // P)
        for t in range(n):
            c0 = max(q0, P * t)
            out.append((k, t, h, t, c0, q1 - c0, t == n - 1))
    return out


TILES = probability_tiles()
NTILE = len(TILES)
TILES_TO = [sum(x[0] <= k for x in TILES) for k in range(GROUPS)]
ITEM_AT = {3: [0, 1, 2], 6: [0, 2, 4], 9: [0, 3, 6]}


def group_size(k):
    return sum(x[0] == k for x in TILES)


class Banks:

    def __init__(self):
        self.n, self.at, self.per = [0] * 8, None, [0] * 8

    def loop(self, register, per):
        self.base, self.at, self.per = list(self.n), register, per

    def end(self, times):
        assert [a - b for a, b in zip(self.n, self.base)] == self.per, (self.n, self.base, self.per)
        self.n = [b + times * p for b, p in zip(self.base, self.per)]
        self.at, self.per = None, [0] * 8

    def before(self, b):
        return self.n[b] + (self.at * self.per[b] if self.at is not None and self.per[b] else 0)

    def after(self, b):
        return self.n[b] + 1 + (self.at * self.per[b] if self.at is not None and self.per[b] else 0)

    def use(self, b):
        self.n[b] += 1


XT_BANKS = [(2 * t + g) % 8 for t in range(NT) for g in range(2)]
K_TURN, V_TURN = [6, 7, 6], [7, 3, 4]
PAIR_PER = [2, 2, 2, 2, 2, 1, 2, 2]
G_LG, G_KTURN, G_VTURN = [6, 7, 6], [6, 7, 6], [[7, 6, 7], [6, 7, 6]]
G_VB, G_OS = [6, 7, 6, 7], 6
GLA_PER = [9, 4, 8, 4, 9, 8, 15, 11]
FFN_PER = [5, 5, 5, 5, 5, 5, 3, 3]
MEAN_BANKS, SQ_BANKS = [6, 7, 6], [7, 6, 7]
A3, B3 = [0, 1, 2], [3, 4, 5]
OUT_BANKS = [6, 7, 0, 1, 2, 3, 4, 5]
SILU = ACT.Silu
KV_STORES = 6


def build(nc, IN, OUT):
    es = ExitStack()
    with es:
        sems = {}

        def sem(name):
            if name not in sems:
                sems[name] = es.enter_context(nc.semaphore(name))
            return sems[name]

        bank_full = [sem(f"bank_full{b}") for b in range(8)]
        bank_free = [sem(f"bank_free{b}") for b in range(8)]
        raw_loaded = [sem(f"raw_loaded{s}") for s in range(RING)]
        psum = es.enter_context(nc.psum_tensor("psum", [P, 8, 512], F32))

        top = [-(-nc.sbuf_base // 32) * 32]

        def size(shape, dt):
            n = int(np.prod(shape[1:])) * (2 if dt == BF16 else 4)
            return -(-n // 32) * 32

        def keep(name, shape, dt=F32):
            t = nc.alloc_sbuf_tensor_at(name, shape, dt, offset=top[0])
            top[0] += size(shape, dt)
            return t

        def region(offset, limit):
            at = [offset]

            def put(name, shape, dt=F32):
                t = nc.alloc_sbuf_tensor_at(name, shape, dt, offset=at[0])
                at[0] += size(shape, dt)
                assert at[0] <= offset + limit, (name, at[0] - offset, limit)
                return t
            return put

        raw = keep("raw", [P, RING, D])
        wh, wl = keep("wh", [P, RING, D], F32R), keep("wl", [P, RING, D], F32R)
        xh, xl = keep("xh", [P, KT, T], F32R), keep("xl", [P, KT, T], F32R)
        ident = keep("ident", [P, P])
        identr = keep("identr", [P, P], F32R)
        ones = keep("ones", [P, P])
        onesr = keep("onesr", [2, P], F32R)
        tri = keep("tri", [P, P])
        lnp = keep("lnp", [P, 4, KT])
        gng = keep("gng", [P, 1])
        bfc = keep("bfc", [FH, 1])
        bac = keep("bac", [P, 2])
        pages = keep("pages", [1, NB * NPAGE], I32)
        eps = keep("eps", [P, 2])
        OHB = top[0]
        oh = keep("oh", [P, 8, T], F32R)
        OLB = top[0]
        ol = keep("ol", [P, 8, T], F32R)
        R1 = top[0]
        R1N = (nc.sbuf_usable_end - R1) // 32 * 32
        HALF = 4 * T * 4
        EARLY, WA = size([P, P], F32) + 3 * size([P, P], BF16), size([RANK, GK], F32)
        e = region(R1 + R1N - EARLY - WA, EARLY + WA)
        low = e("low", [P, P])
        identb = e("identb", [P, P], BF16)
        later = e("later", [P, P], BF16)
        early = e("early", [P, P], BF16)
        wa2 = e("wa2", [RANK, GK])
        RE = R1 + R1N - EARLY - WA
        at_a = lambda: region(OHB + HALF, HALF)
        at_b = lambda: region(OLB + HALF, HALF)
        at_c = lambda: region(R1, RE - R1)

        xstage, xlast = at_c()("xstage", [P, 8, D]), at_a()("xlast", [TAIL + NB, D])
        a, b = at_a(), at_b()
        fz, fe, lfT = a("fz", [FH, T]), a("fe", [FH, T]), a("lfT", [FH, T])
        negc, lones = b("negc", [FH, TP]), b("lones", [FH, TP])
        a, b, c = at_a(), at_b(), at_c()
        alrT = c("alrT", [RANK, T])
        sq_tok, sk_tok, sv_tok = c("sq_tok", [NB, FW]), c("sk_tok", [NB, FW]), c("sv_tok", [NB, FW])
        svT = c("svT", [P, 4, NB])
        slf = c("slf", [NB, FH])
        C_AFTER = R1 + size([P, T], F32) + 3 * size([NB, FW], F32) + 128 + 32
        qh, ql, kh, kl = (a(x, [P, T], F32R) for x in ("qh", "ql", "kh", "kl"))
        cb, vh, vl = b("cb", [P, 2, TP]), b("vh", [P, T], F32R), b("vl", [P, T], F32R)
        vx, k_tok = c("vx", [P, NT, 3 * DH]), c("k_tok", [P, NT, P])
        pt, of = c("pt", [P, 3, SEG]), c("of", [P, 2, SEG])
        nmT = c("nmT", [2, 2, SEG], F32R)
        nmax, nms = c("nmax", [P, NI]), c("nms", [P, NI, 2], F32R)
        negc_tok, nck = c("negc_tok", [P, NT, FH]), c("nck", [P, NT, 2])
        lf_tok = c("lf_tok", [P, NT, FH])
        a, b, c = at_a(), at_b(), region(C_AFTER, RE - C_AFTER)
        kv = [a("kv0", [P, NPAGE, FW]), b("kv1", [P, NPAGE, FW]), c("kv2", [P, NPAGE, FW])]
        ss = c("ss", [P, NB, NPAGE, FH])
        lfp = c("lfp", [P, NB, NPAGE, FH])
        lfs = nc.alloc_sbuf_tensor_at("lfs", [P, NB, NPAGE, FH], F32, offset=RE - 2048 - 32 * 80)
        rest = region(RE - 32 * 80, 32 * 80)
        sqk = nc.alloc_sbuf_tensor_at("sqk", [NB, FW], F32, offset=RE - 2048 - 32 * 80)
        dself, sbc, mbc = rest("dself", [NB, NB, FH]), rest("sbc", [P, NB, FH]), rest("mbc", [P, NB, FH])
        mx, mcol, dmx = rest("mx", [P, NB, FH]), rest("mcol", [64, 1]), rest("dmx", [64, 64])
        den, spr = rest("den", [P, NB, FH]), rest("spr", [P, NB, FH])
        sself = rest("sself", [NB, FH])
        onum = rest("onum", [P, 4, NB])
        gated = nc.alloc_sbuf_tensor_at("gated", [P, 4, T], F32, offset=R1 + R1N - WA - HALF)
        a, b, c = at_a(), at_b(), region(R1 + size([P, T], F32), R1N - WA - HALF - size([P, T], F32))
        qe, ke, go = a("qe", [P, T]), a("ke", [P, T]), a("go", [P, 2, T])
        gx, gy = b("gx", [P, T]), b("gy", [P, T])
        gsq = nc.alloc_sbuf_tensor_at("gsq", [P, 2, T], F32, offset=OLB + HALF)
        sst = b("sst", [P, NB, P])
        gsc = b("gsc", [P, 2, 2, P])
        stt, kvs, stp = b("stt", [P, P]), b("kvs", [P, P]), c("stp", [P, 2, 2, P])
        vb_tok, ke_tok = c("vb_tok", [P, NT, 2 * P]), c("ke_tok", [P, NT, P])
        gvT = nc.alloc_sbuf_tensor_at("gvT", [P, T], F32, offset=OHB + HALF + 2 * size([P, T], F32))
        gl, eg, vs_tok = c("gl", [P, 3, NT]), c("eg", [P, NB]), b("vs_tok", [NB, 2 * P])
        wai, bai = c("wai", [RANK, P]), c("bai", [P, 1])
        c = region(R1, R1N)
        mixed = c("mixed", [P, KT, T])
        sgb = c("sgb", [P, T])
        ysum = nc.alloc_sbuf_tensor_at("ysum", [P, T], F32, offset=R1 + KT * T * 4)
        z = region(OHB, 16 * T * 4)
        hh, hl = z("hh", [P, 2, T], F32R), z("hl", [P, 2, T], F32R)
        sg, hf = z("sg", [P, 2, T]), z("hf", [P, 2, 352])
        ysq, yrst = z("ysq", [P, 2, KT, 352]), z("yrst", [P, T])
        yout = z("yout", [P, 2, D])
        negc_dram = nc.dram_tensor("negc_scratch", [FH, TP], F32, kind="Internal").ap()

        def bank(b):
            return psum[:, b, :]

        def wt(buf, slot, k):
            return buf[:, slot, k * P:(k + 1) * P]

        def f(ap):
            return ap.bitcast(F32)

        def apart(engine):
            engine.sem_inc(sem(f"apart_{str(engine.engine).split('.')[-1]}"), 1)

        w_in = IN["w_in"][0]
        block = es.enter_context(nc.Block())

        @block.sync
        def _(sp):
            def small(dst, src):
                sp.dma_start(dst, src, allow_slow_non_contiguous=True).then_inc(sem("params_loaded"), 16)

            def halves(slot, parts):
                for dst, src in parts:
                    sp.dma_start(dst, src).then_inc(raw_loaded[slot], 16)

            def columns(slot, w, col):
                src = w.rearrange("(k p) n -> p k n", p=P)
                dst = raw[:, slot, :].rearrange("p (k n) -> p k n", n=P)
                halves(slot, [(dst[:, 4 * m:4 * m + 4, :], src[:, 4 * m:4 * m + 4, bass.ds(col, P)])
                              for m in range(2)])

            def panel_free(p):
                if isinstance(p, int) and p < RING:
                    return
                sp.wait_ge(sem("panel_split"), p - RING + 1)
                if not isinstance(p, int):
                    apart(sp)

            for t in range(NT):
                rows = P if t < 8 else TAIL + NB
                if t == 0:
                    sp.dma_start(xstage[0:META, 0, :], IN["meta"]).then_inc(sem("x_loaded0"), 16)
                    sp.dma_start(xstage[META:P, 0, :], IN["x_prompt"][0, 0:P - META, :])\
                        .then_inc(sem("x_loaded0"), 16)
                elif t < 8:
                    sp.dma_start(xstage[:, t, :], IN["x_prompt"][0, P * t - META:P * t + P - META, :])\
                        .then_inc(sem(f"x_loaded{t}"), 16)
                else:
                    sp.dma_start(xlast[0:TAIL, :], IN["x_prompt"][0, SEQ - TAIL:SEQ, :])\
                        .then_inc(sem("x_loaded8"), 16)
                    sp.dma_start(xlast[TAIL:TAIL + NB, :], IN["x_sample"][:, 0, :])\
                        .then_inc(sem("x_loaded8"), 16)
            sp.wait_ge(sem("narrow_zeroed"), 1)
            src = w_in.rearrange("(k p) n -> p k n", p=P)
            dst = raw[:, 0, :].rearrange("p (k n) -> p k n", n=P)
            halves(0, [(dst[:, :, 0:FH], src[:, :, O_FA:O_FA + FH]),
                       (dst[:, :, ROW_ALR:ROW_ALR + RANK], src[:, :, O_AL:O_AL + RANK])])
            columns(1, w_in, 0)
            columns(2, w_in, FW)
            for m, name in enumerate(["ln1_g", "ln1_b", "ln2_g", "ln2_b"]):
                small(lnp[:, m, :], IN[name][0].rearrange("(k p) -> p k", p=P))
            small(gng[:, :], IN["gla_norm_g"][0].rearrange("(p a) -> p a", a=1))
            small(bfc[:, :], IN["b_f"][0].rearrange("(p a) -> p a", a=1))
            small(wa2[:, :], IN["w_a2"][0])
            small(bac[:, :], IN["b_a"][0].rearrange("(k p) -> p k", p=P))
            small(pages[:, :], IN["page_table"].rearrange("(a b) p -> a (b p)", a=1))
            panel_free(3)
            columns(0, w_in, 2 * FW)

            def spread(j):
                sp.dma_start(cb[:, :, :], negc_dram[bass.ds(2 * j, 2), :].partition_broadcast(P))\
                    .then_inc(sem("cb_loaded"), 16)
            sp.wait_ge(sem("negc_ready"), 1)
            sp.dma_start(negc_dram, negc[:, :]).then_inc(sem("negc_stored"), 16)
            sp.wait_ge(sem("negc_stored"), 16)
            sp.wait_ge(sem("negc_turned"), 1)
            spread(0)
            with sp.Fori(1, 4) as j:
                for m in range(3):
                    panel_free(PAN_QKV + 3 * j + m)
                    columns((1 + m) % RING, w_in, FW * m + P * j)
                sp.wait_ge(sem("scores_read"), NI * j)
                apart(sp)
                spread(j)

            sp.wait_ge(sem("params_loaded"), 16 * 9)
            sp.wait_ge(sem("o_done"), 1)
            sp.wait_ge(sem("kv_stored"), KV_STORES * 16 * 4)
            def page(n, p):
                at = n * NPAGE + p
                return sp.value_load(pages[0:1, at:at + 1], min_val=0, max_val=NPOOL - 1)

            def fill(n):
                cache = IN["cache_k"][0] if n < NB else IN["cache_v"][0]
                if n >= 3:
                    sp.wait_ge(sem("kv_used"), n - 2)
                for p in range(NPAGE):
                    sp.dma_start(kv[n % 3][:, p, :],
                                 cache[bass.ds(page(n % NB, p), 1), :, :, :].rearrange("a k h d -> (a k) (h d)"))\
                        .then_inc(sem(f"kv_loaded{n % 3}"), 16)
            for n in range(3):
                fill(n)
            for n in range(NB):
                for p in range(NPAGE):
                    sp.dma_start(lfp[:, n, p, :],
                                 IN["cache_lf"][0][bass.ds(page(n, p), 1), :, :].rearrange("a k h -> (a k) h"))\
                        .then_inc(sem("lf_loaded"), 16)
            for n in range(3, 2 * NB):
                fill(n)

            def state_load(i):
                for hh_ in range(2):
                    sp.dma_start(sst[64 * hh_:64 * hh_ + 64, :, :],
                                 IN["state_gla"][0][:, bass.ds(2 * i + hh_, 1), :, :]
                                 .rearrange("b h d v -> d (b h) v")).then_inc(sem("sst_loaded"), 16)
            def gla_panels(i):
                for m, col in enumerate([O_QB + P * i, O_KB + P * i, O_VB + 2 * P * i, O_VB + 2 * P * i + P,
                                         O_RB + 2 * P * i, O_RB + 2 * P * i + P]):
                    panel_free(PAN_GLA + 6 * i + m)
                    columns((1 + m) % RING, w_in, col)
            for m, col in enumerate([O_QB, O_KB, O_VB]):
                panel_free(PAN_GLA + m)
                columns((1 + m) % RING, w_in, col)
            sp.wait_ge(sem("samples_done"), 1)
            state_load(0)
            for m, col in enumerate([O_VB + P, O_RB, O_RB + P]):
                panel_free(PAN_GLA + 3 + m)
                columns((1 + m) % RING, w_in, col)
            gla_panels(1)
            sp.wait_ge(sem("sst_stored"), 32)
            state_load(1)

            def merge_panels(m):
                panel_free(PAN_MERGE + 3 * m)
                columns(1, w_in, O_GA + P * m)
                panel_free(PAN_MERGE + 3 * m + 1)
                columns(2, w_in, O_GB + P * m)
                panel_free(PAN_MERGE + 3 * m + 2)
                dst = raw[:, 0, :].rearrange("p (k n) -> p k n", n=P)
                halves(0, [(dst[:, 4 * g:4 * g + 4, :],
                            IN[name][0].rearrange("(k p) n -> p k n", p=P)[:, :, bass.ds(P * m, P)])
                           for g, name in enumerate(["w_pa", "w_pb"])])
            with sp.Fori(0, KT) as m:
                merge_panels(m)
            for m in range(8):
                panel_free(PAN_O + m)
                columns((PAN_O + m) % RING, IN["w_o"][0], P * m)
            with sp.Fori(0, FGROUPS) as g:
                for m in range(4):
                    panel_free(PAN_FFN + 6 * g + m)
                    columns(m % RING, IN["w_up" if m % 2 else "w_gate"][0], 2 * P * g + P * (m // 2))
                for m in range(2):
                    panel_free(PAN_FFN + 6 * g + 4 + m)
                    slot = (4 + m) % RING
                    dst = raw[:, slot, :].rearrange("p (k n) -> p k n", k=2)
                    src = IN["w_down"][0][bass.ds(2 * P * g, 2 * P), :].rearrange("(k p) n -> p k n", p=P)
                    halves(slot, [(dst[:, k, :], src[:, k, 512 * m:512 * m + 512]) for k in range(2)])

        @block.gpsimd
        def _(pool):
            pool.memset(raw[:, 0, :], 0.0).then_inc(sem("narrow_zeroed"), 1)
            made = sem("made")
            pool.memset(ident[:, :], 0.0).then_inc(made, 1)
            pool.memset(ones[:, :], 1.0).then_inc(made, 1)
            pool.memset(later[:, :], 0.0).then_inc(made, 1)
            pool.wait_ge(made, 3)
            pool.affine_select(out=ident[:, :], in_=ident[:, :], compare_op=ALU.not_equal, fill=1.0, base=0,
                               pattern=[[-1, P]], channel_multiplier=1).then_inc(sem("ident_ready"), 1)
            pool.wait_ge(sem("ident_ready"), 1)
            pool.affine_select(out=tri[:, :], in_=ones[:, :], compare_op=ALU.is_ge, fill=0.0, base=0,
                               pattern=[[1, P]], channel_multiplier=-1).then_inc(made, 1)
            pool.wait_ge(made, 4)
            pool.affine_select(out=low[:, :], in_=ones[:, :], compare_op=ALU.is_gt, fill=0.0, base=0,
                               pattern=[[-1, P]], channel_multiplier=1).then_inc(made, 1)
            pool.wait_ge(made, 5)
            pool.tensor_copy(identb[:, :], ident[:, :]).then_inc(made, 1)
            pool.wait_ge(made, 6)
            pool.tensor_copy(early[:, :], later[:, :]).then_inc(made, 1)
            pool.wait_ge(made, 7)
            pool.affine_select(out=later[:, :], in_=later[:, :], compare_op=ALU.is_ge, fill=NEG, base=0,
                               pattern=[[-1, P]], channel_multiplier=1).then_inc(made, 1)
            pool.wait_ge(made, 8)
            pool.affine_select(out=early[:, :], in_=early[:, :], compare_op=ALU.is_ge, fill=NEG, base=0,
                               pattern=[[1, P]], channel_multiplier=-1).then_inc(made, 1)
            pool.wait_ge(made, 9)
            pool.tensor_copy(identr[:, :], ident[:, :]).then_inc(made, 1)
            pool.wait_ge(made, 10)
            pool.tensor_copy(onesr[:, :], ones[0:2, :]).then_inc(made, 1)
            pool.wait_ge(made, 11)
            pool.memset(eps[:, 0:1], 1e-6).then_inc(made, 1)
            pool.memset(eps[:, 1:2], 1e-5).then_inc(sem("consts_ready"), 1)

            def split(s, use, p):
                pool.wait_ge(raw_loaded[s], 32 * use)
                if not (isinstance(p, int) and p < RING):
                    pool.wait_ge(sem("panel_used"), p - RING + 1)
                apart(pool)
                pool.tensor_copy(wh[:, s, :], raw[:, s, :]).then_inc(sem("panel_high"), 1)
                pool.wait_ge(sem("panel_high"), p + 1)
                pool.tensor_tensor(wl[:, s, :], raw[:, s, :], f(wh[:, s, :]), ALU.subtract)\
                    .then_inc(sem("panel_split"), 1)
            for s in range(RING):
                split(s, 1, s)
            with pool.Fori(1, PANELS // RING) as i:
                for s in range(RING):
                    split(s, i + 1, RING * i + s)

        @block.tensor
        def _(pe):
            B = Banks()
            mm = nc.tensor.matmul

            def take(b):
                if isinstance(B.before(b), int) and B.before(b) == 0:
                    return
                pe.wait_ge(bank_free[b], B.before(b))

            def give(b, ins):
                ins.then_inc(bank_full[b], 1)
                B.use(b)

            def settled(b):
                pe.wait_ge(bank_free[b], B.before(b))

            def job(p, slot, banks, ks, xs, release=True, before_chunk=None):
                if p is not None:
                    pe.wait_ge(sem("panel_split"), p + 1)
                for c, (c0, cw) in enumerate(CHUNKS):
                    b = banks[c]
                    take(b)
                    if before_chunk is not None:
                        before_chunk(c)
                    out = psum[:, b, 0:cw]
                    for n, k in enumerate(ks):
                        w = (wt(wh, slot, k), wt(wl, slot, k))
                        x = [h[:, xs[1][n], c0:c0 + cw] for h in xs[0]]
                        first = mm(out, w[0], x[0], start=(n == 0), stop=False)
                        if release and c == 0 and n == 0:
                            first.then_inc(sem("panel_used"), 1)
                        mm(out, w[0], x[1], start=False, stop=False)
                        last = mm(out, w[1], x[0], start=False, stop=(n == len(ks) - 1))
                    give(b, last)

            X8 = ((xh, xl), list(range(8)))
            ALL8 = list(range(8))

            pe.wait_ge(sem("ident_ready"), 1)
            for t in range(NT):
                rows = P if t < 8 else TAIL + NB
                pe.wait_ge(sem(f"x_loaded{t}"), 32 if t in (0, 8) else 16)
                src = xstage[0:rows, t, :] if t < 8 else xlast[:, :]
                for g in range(2):
                    b = XT_BANKS[2 * t + g]
                    take(b)
                    for k in range(4):
                        last = nc.tensor.transpose(psum[:, b, k * P:k * P + rows],
                                                   src[:, (4 * g + k) * P:(4 * g + k + 1) * P],
                                                   ident[0:rows, 0:rows])
                    give(b, last)
            pe.wait_ge(sem("consts_ready"), 1)

            for b in range(8):
                settled(b)
            job(0, 0, A3, ALL8, X8, release=False)
            take(3)
            pe.wait_ge(sem("lf_ready"), 1)
            for t in range(NT):
                w = width(t)
                nc.tensor.transpose(psum[0:w, 3, t * FH:(t + 1) * FH], lfT[:, t * P:t * P + w],
                                    ident[0:FH, 0:FH])
            last = nc.tensor.transpose(psum[0:NB, 3, NT * FH:(NT + 1) * FH], lfT[:, TP:T], ident[0:FH, 0:FH])
            give(3, last)
            take(4)
            pe.wait_ge(sem("negc_ready"), 1)
            for t in range(NT):
                w = width(t)
                last = nc.tensor.transpose(psum[0:w, 4, t * FH:(t + 1) * FH], negc[:, t * P:t * P + w],
                                           ident[0:FH, 0:FH])
            give(4, last)

            def turn(parts, banks, extra):
                def one(out, src, cols):
                    if len(src) == 1:
                        return nc.tensor.transpose(out, src[0][:, cols], ident[:, :])
                    mm(out, src[0][:, cols], identr[:, :], start=True, stop=False)
                    return mm(out, src[1][:, cols], identr[:, :], start=False, stop=True)
                for g, b in enumerate(banks):
                    take(b)
                    for t in range(4 * g, min(4 * g + 4, NT)):
                        w = width(t)
                        last = one(psum[0:w, b, (t - 4 * g) * P:(t - 4 * g + 1) * P], parts,
                                   slice(t * P, t * P + w))
                    if g == 2:
                        for m, e in enumerate(extra):
                            last = one(psum[0:NB, b, (m + 1) * P:(m + 2) * P], e, slice(TP, T))
                    give(b, last)

            with pe.Fori(0, 4) as j:
                B.loop(j, PAIR_PER)
                p = PAN_QKV + 3 * j
                job(p, 1, A3, ALL8, X8)
                job(p + 1, 2, B3, ALL8, X8)
                job(p + 2, 0, A3, ALL8, X8)

                def scores(n):
                    h, i = divmod(n, NT)
                    nq, nk = width(i), min(P * (i + 1), TP)
                    rows = slice(DH * h, DH * h + DH)
                    if n > 0:
                        pe.wait_ge(sem("scores_read"), NI * j + n)
                        if nq < P:
                            apart(pe)
                    for c0 in range(0, nk, 512):
                        c1 = min(c0 + 512, nk)
                        last = mm(psum[0:nq, c0 // 512, 0:c1 - c0], qh[rows, i * P:i * P + nq],
                                  kh[rows, c0:c1], start=True, stop=(c1 != nk))
                    d0 = i * P - c0
                    last = mm(psum[0:nq, c0 // 512, d0:d0 + nq], identb[0:nq, 0:nq], later[0:nq, 0:nq],
                              start=False, stop=True)
                    last.then_inc(sem("scores_full"), 1)

                def group_scores(k):
                    for n in range(PER_SEG * k, PER_SEG * k + PER_SEG):
                        scores(n)

                def rows_of(k):
                    if k > 0:
                        pe.wait_ge(sem("rows_ready"), GROUPS * j + k)
                    pe.wait_ge(sem("max_split"), GROUPS * j + k + 1)
                    for q in range(PER_SEG):
                        n = PER_SEG * k + q
                        nq = width(n % NT)
                        if nq < P:
                            apart(pe)
                        last = mm(psum[0:2, 7, q * P:q * P + nq], nms[0:nq, n, :], identr[0:nq, 0:nq],
                                  start=True, stop=True)
                    last.then_inc(sem("rows_full"), 1)

                def tile_scores(x):
                    k, l, h, t, c0, n, _ = TILES[x]
                    rows, w, b = slice(DH * h, DH * h + DH), width(t), 3 + x % 2
                    if x >= 2:
                        pe.wait_ge(sem("probs_ready"), NTILE * j + x - 1)
                    if l == 0:
                        pe.wait_ge(sem("rows_ready"), GROUPS * j + k + 1)
                    if w < P:
                        apart(pe)
                    out, off = psum[0:w, b, 0:n], c0 % SEG
                    keys, queries = slice(P * t, P * t + w), slice(c0, c0 + n)
                    mm(out, kh[rows, keys], qh[rows, queries], start=True, stop=False)
                    mm(out, kh[rows, keys], ql[rows, queries], start=False, stop=False)
                    mm(out, kl[rows, keys], qh[rows, queries], start=False, stop=False)
                    diagonal = c0 == P * t
                    last = mm(out, onesr[:, 0:w], nmT[:, k % 2, off:off + n], start=False, stop=not diagonal)
                    if diagonal:
                        m = min(P, n)
                        last = mm(psum[0:w, b, 0:m], identb[0:w, 0:w], early[0:w, 0:m], start=False,
                                  stop=True)
                    last.then_inc(sem("tile_full"), 1)

                def mix(x):
                    k, l, h, t, c0, n, end = TILES[x]
                    w, b, off = width(t), 5 + k % 2, c0 % SEG
                    if l == 0 and k >= 2:
                        pe.wait_ge(sem("o_read"), GROUPS * j + k - 1)
                    pe.wait_ge(sem("probs_ready"), NTILE * j + x + 1)
                    if w < P:
                        apart(pe)
                    last = mm(psum[:, b, off:off + n], vx[0:w, t, DH * h:DH * h + P], pt[0:w, x % 3, 0:n],
                              start=(t == 0), stop=end)
                    last.then_inc(sem("mixed_in"), 1)

                for b in B3:
                    settled(b)
                turn((kh, kl), K_TURN, [(kh, kl), (qh, ql)])
                for b in A3:
                    settled(b)
                group_scores(0)
                turn((vh, vl), V_TURN, [(vh, vl)])
                group_scores(1)
                for b in range(8):
                    settled(b)
                rows_of(0)
                for x in range(NTILE):
                    k, l = TILES[x][0:2]
                    tile_scores(x)
                    if k + 2 < GROUPS and l in ITEM_AT[group_size(k)]:
                        scores(PER_SEG * (k + 2) + ITEM_AT[group_size(k)].index(l))
                    if k + 1 < GROUPS and l == 1:
                        rows_of(k + 1)
                    if x > 0:
                        mix(x - 1)
                mix(NTILE - 1)
                pe.wait_ge(sem("o_read"), GROUPS * j + GROUPS)
                B.end(4)

            for n in range(NB):
                b = n % 2
                take(b)
                settled(6)
                last = mm(bank(b), ident[0:NB, n:n + 1].to_broadcast([NB, P]), sq_tok[:, :], start=True,
                          stop=True)
                give(b, last)
            take(2)
            pe.wait_ge(sem("dself_ready"), 1)
            last = mm(psum[:, 2, 0:64], ones[0:NB, :], dself[:, :, :].rearrange("a b h -> a (b h)"),
                      start=True, stop=True)
            give(2, last)
            take(3)
            pe.wait_ge(sem("dself_ready"), 2)
            pe.wait_ge(sem("lfs_ready"), 1)
            pe.wait_ge(sem("lf_loaded"), 16 * NB * NPAGE)
            flat = lambda t: t[:, :, :, :].rearrange("q b p h -> q (b p h)")
            mm(bank(3), ones[:, :], flat(lfs), start=True, stop=False)
            mm(bank(3), low[:, :], flat(lfp), start=False, stop=False)
            last = mm(psum[:, 3, :].rearrange("q (b p h) -> q b p h", b=NB, p=NPAGE), ones[0:NB, :],
                      dself[:, :, :].unsqueeze(2).to_broadcast([NB, NB, NPAGE, FH]), start=False, stop=True)
            give(3, last)
            take(4)
            pe.wait_ge(sem("mx_ready"), 1)
            last = nc.tensor.transpose(psum[0:64, 4, 0:P], mx[:, :, :].rearrange("q b h -> q (b h)"), ident[:, :])
            give(4, last)
            take(5)
            pe.wait_ge(sem("dmx_ready"), 1)
            last = mm(psum[:, 5, 0:64], ones[0:64, :], dmx[:, :], start=True, stop=True)
            give(5, last)
            take(6)
            pe.wait_ge(sem("sprobs_ready"), 2)
            last = mm(bank(6), ones[:, :], flat(ss), start=True, stop=True)
            give(6, last)
            take(7)
            for n in range(NB):
                f_ = NB + n
                pe.wait_ge(sem(f"kv_loaded{f_ % 3}"), 16 * NPAGE * (f_ // 3 + 1))
                for m in range(4):
                    for p in range(NPAGE):
                        o = psum[:, 7, (m * NB + n) * 2:(m * NB + n) * 2 + 2]
                        last = mm(o, kv[f_ % 3][:, p, m * P:(m + 1) * P], ss[:, n, p, 2 * m:2 * m + 2],
                                  start=(p == 0), stop=(p == NPAGE - 1))
                if n < NB - 1:
                    last.then_inc(sem("kv_used"), 1)
            give(7, last)

            with pe.Fori(0, 2) as i:
                B.loop(i, GLA_PER)
                p = PAN_GLA + 6 * i
                pe.wait_ge(sem("wai_ready"), 2 * i + 2)
                for c, (c0, cw) in enumerate(CHUNKS):
                    take(G_LG[c])
                    last = mm(psum[:, G_LG[c], 0:cw], wai[:, :], alrT[:, c0:c0 + cw], start=True, stop=True)
                    give(G_LG[c], last)
                job(p, 1, A3, ALL8, X8)
                job(p + 1, 2, B3, ALL8, X8)
                job(p + 2, 0, A3, ALL8, X8)
                for b in B3:
                    settled(b)
                turn((ke,), G_KTURN, [])
                job(p + 3, 1, B3, ALL8, X8)
                for b in A3:
                    settled(b)
                turn((gvT,), G_VTURN[0], [(gvT,)])
                job(p + 4, 2, A3, ALL8, X8)
                for b in B3:
                    settled(b)
                turn((gvT,), G_VTURN[1], [(gvT,)])
                job(p + 5, 0, B3, ALL8, X8)
                for b in range(8):
                    settled(b)

                def within(c):
                    n, b = width(c), 2 * (c % 2)
                    cols = slice(c * P, c * P + n)
                    take(b)
                    if n < P:
                        apart(pe)
                    for h in range(2):
                        rows = slice(64 * h, 64 * h + 64)
                        last = mm(psum[0:n, b + h, 0:n], ke[rows, cols], qe[rows, cols],
                                  start=True, stop=True)
                    give(b, last)
                    kvb = 6 + c % 2
                    take(kvb)
                    last = mm(psum[:, kvb, 0:2 * P], ke_tok[0:n, c, :], vb_tok[0:n, c, :], start=True, stop=True)
                    give(kvb, last)

                def outputs(c):
                    n, b = width(c), 4 + c % 2
                    take(b)
                    settled(2 * (c % 2))
                    if c > 0:
                        pe.wait_ge(sem("stp_ready"), 8 * i + c)
                    for h in range(2):
                        o = psum[:, b, h * P:h * P + n]
                        last = mm(o, vb_tok[0:n, c, h * P:(h + 1) * P], gsc[0:n, c % 2, h, 0:n], start=True,
                                  stop=(c == 0))
                        if c > 0:
                            last = mm(o, stp[:, c % 2, h, :], qe[:, c * P:c * P + n], start=False, stop=True)
                    give(b, last)
                for c in range(NT + 1):
                    if c < NT:
                        within(c)
                    if c > 0:
                        outputs(c - 1)
                for m in range(4):
                    b = G_VB[m]
                    take(b)
                    for q in range(2):
                        n = 2 * m + q
                        last = mm(psum[:, b, q * 256:(q + 1) * 256], ident[0:NB, n:n + 1].to_broadcast([NB, P]),
                                  vs_tok[:, :], start=True, stop=True)
                    give(b, last)
                take(6)
                take(7)
                pe.wait_ge(sem("sst_ready"), NB * (i + 1))
                for h in range(2):
                    rows = slice(64 * h, 64 * h + 64)
                    for n in range(NB):
                        last = mm(psum[:, G_OS + h, n:n + 1], sst[rows, n, :],
                                  qe[rows, TP + n:TP + n + 1], start=True, stop=True)
                give(G_OS, last)
                for h in range(2):
                    for c, (c0, cw) in enumerate(CHUNKS):
                        b = (A3, B3)[h][c]
                        take(b)
                        if h == 0 and c == 0:
                            for q in (0, 2, 4, 5, 6):
                                settled(q)
                        last = mm(psum[:, b, 0:cw], ones[:, :], gsq[:, h, c0:c0 + cw], start=True, stop=True)
                        give(b, last)
                B.end(2)

            pe.wait_ge(sem("o_split"), 4)
            with pe.Fori(0, KT) as m:
                B.loop(m, [2, 2, 2, 2, 2, 2, 0, 0])
                p = PAN_MERGE + 3 * m
                job(p, 1, A3, ALL8, X8)
                job(p + 1, 2, B3, ALL8, X8)
                job(p + 2, 0, A3, [0, 1, 2, 3], ((oh, ol), [0, 1, 2, 3]))
                job(None, 0, B3, [4, 5, 6, 7], ((oh, ol), [4, 5, 6, 7]), release=False)
                B.end(KT)

            for m in range(KT):
                job(PAN_O + m, (PAN_O + m) % RING, (A3, B3)[m % 2], ALL8, ((oh, ol), ALL8),
                    before_chunk=(lambda c: pe.wait_ge(sem("mixed_split"), 2 * (c + 1))) if m == 0 else None)

            def norm_sums(tag):
                for c, (c0, cw) in enumerate(CHUNKS):
                    b = MEAN_BANKS[c]
                    take(b)
                    pe.wait_ge(sem(f"{tag}_sum"), c + 1)
                    last = mm(psum[:, b, 0:cw], ones[:, :], ysum[:, c0:c0 + cw], start=True, stop=True)
                    give(b, last)
                for c, (c0, cw) in enumerate(CHUNKS):
                    b = SQ_BANKS[c]
                    take(b)
                    for k in range(KT):
                        pe.wait_ge(sem(f"{tag}_sq"), 2 * c + k // 4 + 1)
                        last = mm(psum[:, b, 0:cw], ones[:, :], ysq[:, c % 2, k, 0:cw], start=(k == 0),
                                  stop=(k == KT - 1))
                    give(b, last)
            norm_sums("ln1")

            with pe.Fori(0, FGROUPS) as g:
                B.loop(g, FFN_PER)
                p = PAN_FFN + 6 * g
                x1 = (lambda c: pe.wait_ge(sem("x1_split"), 2 * (c + 1)))
                job(p, 0, A3, ALL8, X8, before_chunk=x1)
                job(p + 1, 1, B3, ALL8, X8)
                job(p + 2, 2, A3, ALL8, X8)
                job(p + 3, 0, B3, ALL8, X8)
                pe.wait_ge(sem("panel_split"), p + 5)
                pe.wait_ge(sem("panel_split"), p + 6)
                for c, (c0, cw) in enumerate(CHUNKS):
                    pe.wait_ge(sem("hidden_split"), 6 * g + 4 + c)
                    for m in range(KT):
                        b = OUT_BANKS[m]
                        take(b)
                        slot = (4 + m // 4) % RING
                        for k in range(2):
                            w = tuple(x[:, slot, k * 512 + (m % 4) * P:k * 512 + (m % 4 + 1) * P] for x in (wh, wl))
                            x = [x[:, k, c0:c0 + cw] for x in (hh, hl)]
                            out = psum[:, b, 0:cw]
                            first = mm(out, w[0], x[0], start=(k == 0), stop=False)
                            if (c, m, k) in ((0, 0, 0), (2, 4, 0)):
                                first.then_inc(sem("panel_used"), 1)
                            mm(out, w[0], x[1], start=False, stop=False)
                            last = mm(out, w[1], x[0], start=False, stop=(k == 1))
                        give(b, last)
                B.end(FGROUPS)

            norm_sums("ln2")
            for t in range(NT):
                c0, w = (META + t * P, P) if t < 8 else (TP, NB)
                pe.wait_ge(sem("ln2_aff"), KT * (1 if c0 + w <= 352 else 2 if c0 + w <= 704 else 3))
                for g in range(2):
                    b = (2 * t + g) % 6
                    take(b)
                    for k in range(4):
                        last = nc.tensor.transpose(psum[0:w, b, k * P:(k + 1) * P],
                                                   mixed[:, 4 * g + k, c0:c0 + w], ident[:, :])
                    give(b, last)


        @block.scalar
        def _(act):
            B = Banks()
            do = nc.scalar.activation

            def filled(b):
                act.wait_ge(bank_full[b], B.after(b))

            def read(b, ins):
                ins.then_inc(bank_free[b], 1)
                B.use(b)

            def settled(b):
                act.wait_ge(bank_free[b], B.before(b))

            def skip(banks):
                for b in banks:
                    B.use(b)

            for n in range(2 * NT):
                t, g, b = n // 2, n % 2, XT_BANKS[n]
                rows = P if t < 8 else TAIL + NB
                filled(b)
                src = bank(b).rearrange("p (k c) -> p k c", k=4)[:, :, 0:rows]
                do(xh[:, 4 * g:4 * g + 4, t * P:t * P + rows], src, ACT.Copy).then_inc(sem("xh_ready"), 1)
                skip([b])
            act.wait_ge(sem("params_loaded"), 16 * 9)
            act.wait_ge(sem("consts_ready"), 1)
            for c, (c0, cw) in enumerate(CHUNKS):
                filled(c)
                do(fz[:, c0:c0 + cw], psum[0:FH, c, 0:cw], ACT.Identity, bias=bfc[:, 0:1])\
                    .then_inc(sem("fz_ready"), 1)
                read(c, do(alrT[:, c0:c0 + cw], psum[ROW_ALR:ROW_ALR + RANK, c, 0:cw], ACT.Copy))
            act.wait_ge(sem("fz_ready"), 3)
            do(fe[:, :], fz[:, :], ACT.Abs).then_inc(sem("fe"), 1)
            act.wait_ge(sem("fe"), 1)
            do(fe[:, :], fe[:, :], ACT.Exp, scale=-1.0).then_inc(sem("fe"), 1)
            act.wait_ge(sem("fe"), 2)
            do(fe[:, :], fe[:, :], ACT.Ln, bias=1.0).then_inc(sem("fe"), 1)
            skip([3, 4])
            settled(3)
            act.wait_ge(sem("slf_ready"), 1)
            lf_out = OUT["lf_prompt"][0, 0]
            act.dma_start(lf_out[0:8 * P, :].rearrange("(t p) h -> p t h", p=P), lf_tok[:, 0:8, :])\
                .then_inc(sem("lf_stored"), 16)
            act.dma_start(lf_out[8 * P:TP, :], lf_tok[0:TAIL, 8, :]).then_inc(sem("lf_stored"), 16)
            act.dma_start(OUT["lf_sample"][0, :, 0, :], slf[:, :]).then_inc(sem("lf_stored"), 16)

            with act.Fori(0, 4) as j:
                B.loop(j, PAIR_PER)
                def high_halves(dst, banks, scale, also=None):
                    for c, (c0, cw) in enumerate(CHUNKS):
                        filled(banks[c])
                        if c == 2 and also is not None:
                            also(banks[c])
                        do(dst[:, c0:c0 + cw], psum[:, banks[c], 0:cw], ACT.Copy, scale=scale)\
                            .then_inc(sem("qkv_high"), 1)
                        B.use(banks[c])
                high_halves(qh, A3, DH ** -0.5)
                high_halves(kh, B3, 1.0)

                def sample_values(b):
                    do(svT[:, bass.ds(j, 1), :], psum[:, b:b + 1, TP - CHUNKS[2][0]:T - CHUNKS[2][0]], ACT.Copy)\
                        .then_inc(sem("svT_ready"), 1)
                high_halves(vh, A3, 1.0, sample_values)
                skip(K_TURN)
                for g, b in enumerate(V_TURN):
                    filled(b)
                    if g < 2:
                        read(b, do(vx[:, 4 * g:4 * g + 4, :].rearrange("p t (b c) -> p t b c", c=DH)[:, :, 0:3:2, :],
                                   bank(b).rearrange("p (t h c) -> p t h c", t=4, h=2), ACT.Copy))
                    else:
                        do(sv_tok[:, bass.ds(P * j, P)], psum[0:NB, b, P:2 * P], ACT.Copy)\
                            .then_inc(sem("sv_ready"), 1)
                        read(b, do(vx[0:TAIL, 8, :].rearrange("p (b c) -> p b c", c=DH)[:, 0:3:2, :],
                                   psum[0:TAIL, b, 0:P].rearrange("p (h c) -> p h c", h=2), ACT.Copy))
                for b in V_TURN + K_TURN:
                    settled(b)
                o = OUT["k_prompt"][0, 0].rearrange("t h d -> t (h d)")
                act.dma_start(o[0:8 * P, bass.ds(P * j, P)].rearrange("(t p) c -> p t c", p=P),
                              k_tok[:, 0:8, :]).then_inc(sem("kv_stored"), 16)
                act.dma_start(o[8 * P:TP, bass.ds(P * j, P)], k_tok[0:TAIL, 8, :])\
                    .then_inc(sem("kv_stored"), 16)
                o = OUT["v_prompt"][0, 0].rearrange("t h d -> t (h d)")
                for h in range(2):
                    act.dma_start(o[0:8 * P, bass.ds(P * j + DH * h, DH)].rearrange("(t p) c -> p t c", p=P),
                                  vx[:, 0:8, 2 * DH * h:2 * DH * h + DH]).then_inc(sem("kv_stored"), 16)
                    act.dma_start(o[8 * P:TP, bass.ds(P * j + DH * h, DH)],
                                  vx[0:TAIL, 8, 2 * DH * h:2 * DH * h + DH]).then_inc(sem("kv_stored"), 16)

                def row_copy(k):
                    act.wait_ge(sem("rows_full"), GROUPS * j + k + 1)
                    n = min(SEG, TP - SEG * (k % SEGS))
                    do(nmT[:, k % 2, 0:n], psum[0:2, 7, 0:n], ACT.Copy).then_inc(sem("rows_ready"), 1)

                def outputs_high(k):
                    act.wait_ge(sem("o_read"), GROUPS * j + k + 1)
                    h, s = divmod(k, SEGS)
                    rows, n = slice(DH * h, DH * h + DH), min(SEG, TP - SEG * s)
                    do(oh[rows, bass.ds(j, 1), SEG * s:SEG * s + n], of[rows, k % 2:k % 2 + 1, 0:n], ACT.Copy)\
                        .then_inc(sem("oh_ready"), 1)

                act.wait_ge(sem("nck_ready"), j + 1)
                row_copy(0)
                for x, (k, l, h, t, c0, n, _) in enumerate(TILES):
                    w = width(t)
                    act.wait_ge(sem("tile_full"), NTILE * j + x + 1)
                    if x >= 3:
                        act.wait_ge(sem("mixed_in"), NTILE * j + x - 2)
                    do(pt[0:w, x % 3, 0:n], psum[0:w, 3 + x % 2, 0:n], ACT.Exp, bias=nck[0:w, t, h:h + 1])\
                        .then_inc(sem("probs_ready"), 1)
                    if k + 1 < GROUPS and l == 1:
                        row_copy(k + 1)
                    if k > 0 and l == 2:
                        outputs_high(k - 1)
                outputs_high(GROUPS - 1)
                act.wait_ge(sem("kv_stored"), KV_STORES * 16 * (j + 1))
                B.end(4)
            act.wait_ge(sem("sv_ready"), 4)
            settled(6)
            act.dma_start(OUT["v_sample"][0, :, 0, :, :].rearrange("b h d -> b (h d)"), sv_tok[:, :])\
                .then_inc(sem("skv_stored"), 16)
            act.dma_start(OUT["k_sample"][0, :, 0, :, :].rearrange("b h d -> b (h d)"), sk_tok[:, :])\
                .then_inc(sem("skv_stored"), 16)

            skip([n % 2 for n in range(NB)] + [2, 3, 4, 5])
            act.wait_ge(sem("sdiff_ready"), 2)
            do(spr[:, :, :], spr[:, :, :], ACT.Exp).then_inc(sem("sprobs_ready"), 1)
            do(ss[:, :, :, :], ss[:, :, :, :], ACT.Exp).then_inc(sem("sprobs_ready"), 1)
            skip([6, 7])

            act.wait_ge(sem("samples_done"), 1)
            with act.Fori(0, 2) as i:
                B.loop(i, GLA_PER)
                act.wait_ge(sem("wai_ready"), 2 * i + 2)
                for c, b in enumerate(G_LG):
                    c0, cw = CHUNKS[c]
                    filled(b)
                    do(gy[:, c0:c0 + cw], psum[:, b, 0:cw], ACT.Abs, bias=bai[:, 0:1])\
                        .then_inc(sem("gy_abs"), 1)
                    B.use(b)
                act.wait_ge(sem("gy_abs"), 3 * i + 3)
                do(gy[:, :], gy[:, :], ACT.Exp, scale=-1.0).then_inc(sem("gy_ln"), 1)
                act.wait_ge(sem("gy_ln"), 2 * i + 1)
                do(gy[:, :], gy[:, :], ACT.Ln, bias=1.0).then_inc(sem("gy_ln"), 1)
                act.wait_ge(sem("lg_ready"), i + 1)
                do(eg[:, :], gx[:, TP:T], ACT.Exp, scale=1.0 / TAU).then_inc(sem("eg_ready"), 1)
                act.wait_ge(sem("gd_ready"), 2 * i + 2)
                do(gy[:, 0:TP], gx[:, 0:TP], ACT.Exp, scale=-1.0 / TAU).then_inc(sem("decays"), 1)
                act.wait_ge(sem("decays"), 3 * i + 1)
                do(gx[:, 0:TP], gx[:, 0:TP], ACT.Exp, scale=1.0 / TAU).then_inc(sem("decays"), 1)
                act.wait_ge(sem("gl_ready"), i + 1)
                do(gl[:, :, :], gl[:, :, :], ACT.Exp, scale=1.0 / TAU).then_inc(sem("decays"), 1)
                skip(A3 + B3)
                for c, (c0, cw) in enumerate(CHUNKS):
                    filled(A3[c])
                    read(A3[c], do(gvT[:, c0:c0 + cw], psum[:, A3[c], 0:cw], ACT.Copy))
                for g, b in enumerate(G_KTURN):
                    filled(b)
                    if g < 2:
                        ins = do(ke_tok[:, 4 * g:4 * g + 4, :], bank(b).rearrange("p (t c) -> p t c", t=4),
                                 ACT.Copy)
                    else:
                        ins = do(ke_tok[0:TAIL, 8, :], psum[0:TAIL, b, 0:P], ACT.Copy)
                    read(b, ins)

                def values_turned(v):
                    for g, b in enumerate(G_VTURN[v]):
                        filled(b)
                        cols = slice(v * P, (v + 1) * P)
                        if g < 2:
                            ins = do(vb_tok[:, 4 * g:4 * g + 4, cols],
                                     bank(b).rearrange("p (t c) -> p t c", t=4), ACT.Copy)
                        else:
                            do(vs_tok[:, cols], psum[0:NB, b, P:2 * P], ACT.Copy).then_inc(sem("vs_ready"), 1)
                            ins = do(vb_tok[0:TAIL, 8, cols], psum[0:TAIL, b, 0:P], ACT.Copy)
                        read(b, ins)

                v1 = [(b, B.after(b)) for b in B3]
                skip(B3)
                values_turned(0)
                for c, (c0, cw) in enumerate(CHUNKS):
                    b, full = v1[c]
                    act.wait_ge(bank_full[b], full)
                    do(gvT[:, c0:c0 + cw], psum[:, b, 0:cw], ACT.Copy).then_inc(bank_free[b], 1)
                for c, (c0, cw) in enumerate(CHUNKS):
                    filled(A3[c])
                    read(A3[c], do(gated[:, bass.ds(2 * i, 1), c0:c0 + cw], psum[:, A3[c]:A3[c] + 1, 0:cw],
                                   SILU))
                values_turned(1)
                for c, (c0, cw) in enumerate(CHUNKS):
                    filled(B3[c])
                    read(B3[c], do(gated[:, bass.ds(2 * i + 1, 1), c0:c0 + cw],
                                   psum[:, B3[c]:B3[c] + 1, 0:cw], SILU))
                for c in range(NT + 1):
                    if c < NT:
                        skip([2 * (c % 2), 6 + c % 2])
                    if c > 0:
                        q, n = c - 1, width(c - 1)
                        b = 4 + q % 2
                        filled(b)
                        src = psum[:, b, 0:2 * P].rearrange("p (h c) -> p h c", h=2)[:, :, 0:n]
                        do(go[:, :, q * P:q * P + n], src, ACT.Copy).then_inc(sem("go_ready"), 1)
                        read(b, do(gsq[:, :, q * P:q * P + n], src, ACT.Square))
                skip(G_VB)
                filled(G_OS)
                src = psum[:, G_OS:G_OS + 2, 0:NB]
                do(go[:, :, TP:T], src, ACT.Copy).then_inc(sem("go_ready"), 1)
                read(G_OS, do(gsq[:, :, TP:T], src, ACT.Square))
                act.wait_ge(sem("state_ready"), NT * i + NT)
                for hh_ in range(2):
                    rows = slice(64 * hh_, 64 * hh_ + 64)
                    act.dma_start(OUT["gla_prompt"][0, 0, bass.ds(2 * i + hh_, 1), :, :]
                                  .rearrange("h d v -> (h d) v"), stt[rows, :]).then_inc(sem("stt_stored"), 16)
                act.wait_ge(sem("sst_ready"), NB * i + NB)
                for hh_ in range(2):
                    rows = slice(64 * hh_, 64 * hh_ + 64)
                    act.dma_start(OUT["gla_sample"][0][:, bass.ds(2 * i + hh_, 1), :, :]
                                  .rearrange("b h d v -> d (b h) v"), sst[rows, :, :])\
                        .then_inc(sem("sst_stored"), 16)
                for h in range(2):
                    for c, (c0, cw) in enumerate(CHUNKS):
                        b = (A3, B3)[h][c]
                        filled(b)
                        read(b, do(gsq[:, h, c0:c0 + cw], psum[:, b, 0:cw], ACT.Sqrt, scale=1.0 / GDV,
                                   bias=eps[:, 0:1]))
                act.wait_ge(sem("stt_stored"), 32 * i + 32)
                act.wait_ge(sem("sst_stored"), 32 * i + 32)
                act.wait_ge(sem("gated_ready"), 2 * i + 2)
                B.end(2)
            for h in range(GH):
                do(oh[:, 4 + h, :], gated[:, h, :], ACT.Copy).then_inc(sem("og_high"), 1)

            with act.Fori(0, KT) as m:
                B.loop(m, [2, 2, 2, 2, 2, 2, 0, 0])
                for c, (c0, cw) in enumerate(CHUNKS):
                    filled(A3[c])
                    if c == 0:
                        act.wait_ge(sem("o_split"), 4)
                    read(A3[c], do(mixed[:, bass.ds(m, 1), c0:c0 + cw], psum[:, A3[c]:A3[c] + 1, 0:cw],
                                   ACT.Sigmoid))
                for c, (c0, cw) in enumerate(CHUNKS):
                    filled(B3[c])
                    read(B3[c], do(sgb[:, c0:c0 + cw], psum[:, B3[c], 0:cw], ACT.Sigmoid))
                skip(A3 + B3)
                act.wait_ge(sem("mixed_ready"), 3 * m + 3)
                B.end(KT)
            for c, (c0, cw) in enumerate(CHUNKS):
                for q in range(2):
                    do(oh[:, 4 * q:4 * q + 4, c0:c0 + cw], mixed[:, 4 * q:4 * q + 4, c0:c0 + cw], ACT.Copy)\
                        .then_inc(sem("mixed_high"), 1)
            for m in range(KT):
                skip((A3, B3)[m % 2])

            def norm(tag, eps_col, gain, shift, high):
                skip(MEAN_BANKS)

                def squares(c):
                    c0, cw = CHUNKS[c]
                    act.wait_ge(sem(f"{tag}_dev"), 2 * c + 1)
                    for q in range(2):
                        if q == 1:
                            act.wait_ge(sem(f"{tag}_dev"), 2 * c + 2)
                        if c == 2 and q == 0:
                            act.wait_ge(sem(f"{tag}_root"), 1)
                        do(ysq[:, c % 2, 4 * q:4 * q + 4, 0:cw], mixed[:, 4 * q:4 * q + 4, c0:c0 + cw],
                           ACT.Square).then_inc(sem(f"{tag}_sq"), 1)

                def root(c):
                    c0, cw = CHUNKS[c]
                    b = SQ_BANKS[c]
                    filled(b)
                    ins = do(yrst[:, c0:c0 + cw], psum[:, b, 0:cw], ACT.Sqrt, scale=1.0 / D,
                             bias=eps[:, eps_col:eps_col + 1])
                    read(b, ins)

                def affine(c):
                    c0, cw = CHUNKS[c]
                    for k in range(KT):
                        if k % 4 == 0:
                            act.wait_ge(sem(f"{tag}_norm"), 2 * c + k // 4 + 1)
                        do(mixed[:, k, c0:c0 + cw], mixed[:, k, c0:c0 + cw], ACT.Identity,
                           scale=lnp[:, gain, k:k + 1], bias=lnp[:, shift, k:k + 1]).then_inc(sem(f"{tag}_aff"), 1)
                    if high:
                        for q in range(2):
                            act.wait_ge(sem(f"{tag}_aff"), KT * c + 4 * q + 4)
                            do(xh[:, 4 * q:4 * q + 4, c0:c0 + cw], mixed[:, 4 * q:4 * q + 4, c0:c0 + cw],
                               ACT.Copy).then_inc(sem("x1_high"), 1)
                squares(0)
                squares(1)
                root(0)
                squares(2)
                affine(0)
                root(1)
                affine(1)
                root(2)
                affine(2)
            norm("ln1", 1, 0, 1, True)
            act.wait_ge(sem("x1_split"), 6)
            for k in range(KT):
                do(mixed[:, k, :], mixed[:, k, :], ACT.Copy, scale=ALPHA).then_inc(sem("y_scaled"), 1)

            with act.Fori(0, FGROUPS) as g:
                B.loop(g, FFN_PER)
                for u in range(2):
                    for c, (c0, cw) in enumerate(CHUNKS):
                        filled(A3[c])
                        read(A3[c], do(sg[:, u, c0:c0 + cw], psum[:, A3[c], 0:cw], SILU))
                    skip(B3)
                    for c, (c0, cw) in enumerate(CHUNKS):
                        n = 3 * u + c
                        act.wait_ge(sem("hidden"), 6 * g + n + 1)
                        do(hh[:, u, c0:c0 + cw], hf[:, n % 2, 0:cw], ACT.Copy).then_inc(sem("hidden_high"), 1)
                for c in range(3):
                    skip(OUT_BANKS)
                B.end(FGROUPS)
            norm("ln2", 1, 2, 3, False)

            y_p, y_s = OUT["y_prompt"][0], OUT["y_sample"][:, 0, :]
            for t in range(NT):
                w = P if t < 8 else NB
                b0, b1 = (2 * t) % 6, (2 * t + 1) % 6
                filled(b0)
                if t >= 2:
                    act.wait_ge(sem(f"y_stored{t % 2}"), 16 * (t // 2))
                read(b0, do(yout[0:w, t % 2, 0:512], psum[0:w, b0, :], ACT.Copy))
                B.use(b1)
                settled(b0)
                settled(b1)
                dst = y_p[t * P:(t + 1) * P, :] if t < 8 else y_s
                act.dma_start(dst, yout[0:w, t % 2, :]).then_inc(sem(f"y_stored{t % 2}"), 16)
            act.wait_ge(sem("y_stored0"), 16 * 5)
            act.wait_ge(sem("y_stored1"), 16 * 4)
            act.wait_ge(sem("lf_stored"), 48)
            act.wait_ge(sem("skv_stored"), 32)

        @block.vector
        def _(dve):
            B = Banks()
            ve = nc.vector

            def filled(b):
                dve.wait_ge(bank_full[b], B.after(b))

            def read(b, ins):
                ins.then_inc(bank_free[b], 1)
                B.use(b)

            def settled(b):
                dve.wait_ge(bank_free[b], B.before(b))

            def skip(banks):
                for b in banks:
                    B.use(b)

            chain = [0]

            def link(ins):
                chain[0] += 1
                ins.then_inc(sem("dve_steps"), 1)
                dve.wait_ge(sem("dve_steps"), chain[0])

            for n in range(2 * NT):
                t, g, b = n // 2, n % 2, XT_BANKS[n]
                rows = P if t < 8 else TAIL + NB
                dve.wait_ge(sem("xh_ready"), n + 1)
                src = bank(b).rearrange("p (k c) -> p k c", k=4)[:, :, 0:rows]
                cols = slice(t * P, t * P + rows)
                read(b, ve.tensor_tensor(xl[:, 4 * g:4 * g + 4, cols], src, f(xh[:, 4 * g:4 * g + 4, cols]),
                                         ALU.subtract))
            skip(A3)
            link(ve.memset(lones[:, :], 1.0))
            for b in range(8):
                settled(b)
            link(ve.memset(vx[:, :, DH:2 * DH], 1.0))
            link(ve.memset(nmax[:, :], 0.0))
            dve.wait_ge(sem("fz_ready"), 3)
            link(ve.tensor_scalar(lfT[:, :], fz[:, :], 0.0, None, ALU.min))
            dve.wait_ge(sem("fe"), 3)
            ve.tensor_tensor(lfT[:, :], lfT[:, :], fe[:, :], ALU.subtract).then_inc(sem("lf_ready"), 1)
            dve.wait_ge(sem("lf_ready"), 1)
            ve.tensor_tensor_scan(negc[:, :], lones[:, :], lfT[:, 0:TP], 0.0, ALU.mult, ALU.subtract)\
                .then_inc(sem("negc_ready"), 1)
            filled(3)
            ve.tensor_copy(slf[:, :], psum[0:NB, 3, NT * FH:(NT + 1) * FH]).then_inc(sem("slf_ready"), 1)
            link(ve.tensor_copy(lf_tok[0:TAIL, 8, :], psum[0:TAIL, 3, 8 * FH:9 * FH]))
            read(3, ve.tensor_copy(lf_tok[:, 0:8, :], psum[:, 3, 0:8 * FH].rearrange("p (t h) -> p t h", h=FH)))
            filled(4)
            link(ve.memset(negc_tok[:, 8, :], 0.0))
            link(ve.tensor_copy(negc_tok[0:TAIL, 8, :], psum[0:TAIL, 4, 8 * FH:9 * FH]))
            read(4, ve.tensor_copy(negc_tok[:, 0:8, :], psum[:, 4, 0:8 * FH].rearrange("p (t h) -> p t h", h=FH)))
            settled(4)
            dve.sem_inc(sem("negc_turned"), 1)

            with dve.Fori(0, 4) as j:
                B.loop(j, PAIR_PER)
                def low_halves(dst, high, banks, n, scale):
                    for c, (c0, cw) in enumerate(CHUNKS):
                        filled(banks[c])
                        dve.wait_ge(sem("qkv_high"), 9 * j + 3 * n + c + 1)
                        read(banks[c], ve.scalar_tensor_tensor(
                            out=dst[:, c0:c0 + cw], in0=psum[:, banks[c], 0:cw], scalar=scale,
                            in1=f(high[:, c0:c0 + cw]), op0=ALU.mult, op1=ALU.subtract))
                low_halves(ql, qh, A3, 0, DH ** -0.5)
                low_halves(kl, kh, B3, 1, 1.0)
                ve.tensor_copy(nck[:, :, :], negc_tok[:, :, bass.ds(2 * j, 2)]).then_inc(sem("nck_ready"), 1)
                low_halves(vl, vh, A3, 2, 1.0)
                for g, b in enumerate(K_TURN):
                    filled(b)
                    if g < 2:
                        ins = ve.tensor_copy(k_tok[:, 4 * g:4 * g + 4, :],
                                             bank(b).rearrange("p (t c) -> p t c", t=4))
                    else:
                        ve.tensor_copy(sk_tok[:, bass.ds(P * j, P)], psum[0:NB, b, P:2 * P])\
                            .then_inc(sem("stok"), 1)
                        ve.tensor_copy(sq_tok[:, bass.ds(P * j, P)], psum[0:NB, b, 2 * P:3 * P])\
                            .then_inc(sem("stok"), 1)
                        ins = ve.tensor_copy(k_tok[0:TAIL, 8, :], psum[0:TAIL, b, 0:P])
                    read(b, ins)
                skip(V_TURN)
                dve.wait_ge(sem("cb_loaded"), 16 * j + 16)

                def maxima(n):
                    h, i = divmod(n, NT)
                    nq, nk = width(i), min(P * (i + 1), TP)
                    dve.wait_ge(sem("scores_full"), NI * j + n + 1)
                    apart(dve)
                    s = psum[0:nq, 0:3, :].rearrange("p b c -> p (b c)")[:, 0:nk]
                    ve.tensor_tensor_reduce(out=s, in0=s, in1=cb[0:nq, h, 0:nk], scale=-1.0, scalar=3e38,
                                            op0=ALU.add, op1=ALU.min, accum_out=nmax[0:nq, n:n + 1])\
                        .then_inc(sem("scores_read"), 1)

                def group_maxima(k):
                    for n in range(PER_SEG * k, PER_SEG * k + PER_SEG):
                        maxima(n)
                    dve.wait_ge(sem("scores_read"), NI * j + PER_SEG * (k + 1))
                    cols = slice(PER_SEG * k, PER_SEG * (k + 1))
                    ve.tensor_copy(nms[:, cols, 0], nmax[:, cols]).then_inc(sem("max_high"), 1)
                    dve.wait_ge(sem("max_high"), GROUPS * j + k + 1)
                    ve.tensor_tensor(nms[:, cols, 1], nmax[:, cols], f(nms[:, cols, 0]), ALU.subtract)\
                        .then_inc(sem("max_split"), 1)

                def outputs(k):
                    h, s = divmod(k, SEGS)
                    rows, sums, n = slice(DH * h, DH * h + DH), slice(DH - DH * h, 2 * DH - DH * h), \
                        min(SEG, TP - SEG * s)
                    dve.wait_ge(sem("mixed_in"), NTILE * j + TILES_TO[k])
                    ve.reciprocal(of[rows, k % 2, 0:n], psum[sums, 5 + k % 2, 0:n]).then_inc(sem("recip"), 1)
                    dve.wait_ge(sem("recip"), GROUPS * j + k + 1)
                    ve.tensor_tensor(of[rows, k % 2, 0:n], of[rows, k % 2, 0:n], psum[rows, 5 + k % 2, 0:n],
                                     ALU.mult).then_inc(sem("o_read"), 1)

                def outputs_low(k):
                    dve.wait_ge(sem("oh_ready"), GROUPS * j + k + 1)
                    h, s = divmod(k, SEGS)
                    rows, n = slice(DH * h, DH * h + DH), min(SEG, TP - SEG * s)
                    cols = slice(SEG * s, SEG * s + n)
                    ve.tensor_tensor(ol[rows, bass.ds(j, 1), cols], of[rows, k % 2:k % 2 + 1, 0:n],
                                     f(oh[rows, bass.ds(j, 1), cols]), ALU.subtract).then_inc(sem("ol_ready"), 1)
                group_maxima(0)
                group_maxima(1)
                for k in range(GROUPS):
                    if k + 2 < GROUPS:
                        group_maxima(k + 2)
                    if k > 0:
                        outputs_low(k - 1)
                    outputs(k)
                outputs_low(GROUPS - 1)
                dve.wait_ge(sem("ol_ready"), GROUPS * (j + 1))
                dve.wait_ge(sem("kv_stored"), KV_STORES * 16 * (j + 1))
                B.end(4)
            dve.sem_inc(sem("o_done"), 1)

            dve.wait_ge(sem("stok"), 8)
            link(ve.tensor_tensor(sqk[:, :], sq_tok[:, :], sk_tok[:, :], ALU.mult))
            link(ve.tensor_reduce(sself[:, :], sqk[:, :].rearrange("b (h d) -> b h d", d=DH), AX, ALU.add))

            def diagonal(src, n):
                ve.tensor_tensor(dself[:, :, :], src[:, :].unsqueeze(1).to_broadcast([NB, NB, FH]),
                                 ident[0:NB, 0:NB].unsqueeze(2).to_broadcast([NB, NB, FH]), ALU.mult)\
                    .then_inc(sem("dself_ready"), 1)
                dve.wait_ge(sem("dself_ready"), n)
            diagonal(sself, 1)
            for n in range(NB):
                b = n % 2
                dve.wait_ge(sem(f"kv_loaded{n % 3}"), 16 * NPAGE * (n // 3 + 1))
                filled(b)
                k = kv[n % 3][:, :, :]
                read(b, ve.tensor_tensor(k, k, bank(b).unsqueeze(1).to_broadcast([P, NPAGE, FW]), ALU.mult))
                settled(b)
                ve.tensor_reduce(ss[:, n, :, :], k.rearrange("q p (h d) -> q p h d", d=DH), AX, ALU.add)\
                    .then_inc(sem("kv_used"), 1)
            dve.wait_ge(sem("lf_loaded"), 16 * NB * NPAGE)
            link(ve.memset(lfs[:, :, :, :], 0.0))
            for p in reversed(range(NPAGE - 1)):
                link(ve.tensor_tensor(lfs[:, :, p, :], lfs[:, :, p + 1, :], lfp[:, :, p + 1, :], ALU.add))
            ve.sem_inc(sem("lfs_ready"), 1)
            dve.wait_ge(sem("kv_used"), NB)
            filled(2)
            read(2, ve.tensor_copy(sbc[:, :, :], psum[:, 2, 0:64].rearrange("q (b h) -> q b h", b=NB)))
            settled(2)
            diagonal(slf, 2)
            filled(3)
            whole = ss[:, :, :, :].rearrange("q b p h -> q (b p h)")
            read(3, ve.tensor_tensor(whole, whole, bank(3), ALU.add))
            settled(3)
            link(ve.tensor_reduce(mx[:, :, :], ss[:, :, :, :].rearrange("q b p h -> q b h p"), AX, ALU.max))
            ve.tensor_tensor(mx[:, :, :], mx[:, :, :], sbc[:, :, :], ALU.max).then_inc(sem("mx_ready"), 1)
            filled(4)
            read(4, ve.tensor_reduce(mcol[:, :], psum[0:64, 4, 0:P], AX, ALU.max))
            settled(4)
            ve.tensor_scalar(dmx[:, :], ident[0:64, 0:64], mcol[:, 0:1], None, ALU.mult)\
                .then_inc(sem("dmx_ready"), 1)
            filled(5)
            read(5, ve.tensor_copy(mbc[:, :, :], psum[:, 5, 0:64].rearrange("q (b h) -> q b h", b=NB)))
            settled(5)
            ve.tensor_tensor(spr[:, :, :], sbc[:, :, :], mbc[:, :, :], ALU.subtract).then_inc(sem("sdiff_ready"), 1)
            ve.tensor_tensor(ss[:, :, :, :], ss[:, :, :, :],
                             mbc[:, :, :].unsqueeze(2).to_broadcast([P, NB, NPAGE, FH]), ALU.subtract)\
                .then_inc(sem("sdiff_ready"), 1)
            filled(6)
            read(6, ve.tensor_reduce(den[:, :, :], bank(6).rearrange("q (b p h) -> q b h p", b=NB, p=NPAGE),
                                     AX, ALU.add))
            settled(6)
            dve.wait_ge(sem("sprobs_ready"), 2)
            link(ve.tensor_tensor(den[:, :, :], den[:, :, :], spr[:, :, :], ALU.add))
            link(ve.reciprocal(den[:, :, :], den[:, :, :]))
            dve.wait_ge(sem("svT_ready"), 4)
            filled(7)
            for hh_ in range(2):
                rows = slice(64 * hh_, 64 * hh_ + 64)
                own = spr[rows, :, :].rearrange("q b (m e) -> q e m b", e=2)[:, hh_, :, :]
                dd = den[rows, :, :].rearrange("q b (m e) -> q e m b", e=2)[:, hh_, :, :]
                po = psum[rows, 7, 0:64].rearrange("q (m b e) -> q e m b", m=4, e=2)[:, hh_, :, :]
                o = onum[rows, :, :]
                link(ve.tensor_tensor(o, own, svT[rows, :, :], ALU.mult))
                if hh_ == 0:
                    link(ve.tensor_tensor(o, po, o, ALU.add))
                else:
                    read(7, ve.tensor_tensor(o, po, o, ALU.add))
                    settled(7)
                link(ve.tensor_tensor(o, o, dd, ALU.mult))
            link(ve.tensor_copy(oh[:, 0:4, TP:T], onum[:, :, :]))
            ve.tensor_tensor(ol[:, 0:4, TP:T], onum[:, :, :], f(oh[:, 0:4, TP:T]), ALU.subtract)\
                .then_inc(sem("samples_done"), 1)
            dve.wait_ge(sem("samples_done"), 1)
            dve.wait_ge(sem("skv_stored"), 32)

            link(ve.memset(stp[:, :, :, :], 0.0))
            with dve.Fori(0, 2) as i:
                B.loop(i, GLA_PER)
                steps = [0]
                PER = 27

                def step(ins, n=None):
                    steps[0] += 1
                    ins.then_inc(sem("gla_steps"), 1)
                    dve.wait_ge(sem("gla_steps"), PER * i + steps[0])
                ve.tensor_copy(wai[:, :], wa2[:, bass.ds(P * i, P)]).then_inc(sem("wai_ready"), 1)
                ve.tensor_copy(bai[:, :], bac[:, bass.ds(i, 1)]).then_inc(sem("wai_ready"), 1)
                dve.wait_ge(sem("wai_ready"), 2 * i + 2)
                for c, b in enumerate(G_LG):
                    c0, cw = CHUNKS[c]
                    filled(b)
                    dve.wait_ge(sem("gy_abs"), 3 * i + c + 1)
                    read(b, ve.tensor_scalar(gx[:, c0:c0 + cw], psum[:, b, 0:cw], bai[:, 0:1], 0.0,
                                             ALU.add, ALU.min))
                settled(6)
                settled(7)
                dve.wait_ge(sem("gy_ln"), 2 * i + 2)
                ve.tensor_tensor(gx[:, :], gx[:, :], gy[:, :], ALU.subtract).then_inc(sem("lg_ready"), 1)
                dve.wait_ge(sem("lg_ready"), i + 1)
                for c in range(NT):
                    cols = slice(c * P, c * P + width(c))
                    step(ve.tensor_tensor_scan(gy[:, cols], ones[:, 0:width(c)], gx[:, cols], 0.0,
                                               ALU.mult, ALU.add))
                full = gy[:, 0:8 * P].rearrange("p (c t) -> p c t", t=P)
                step(ve.tensor_copy(gl[:, 0, 0:8], full[:, :, P - 1]))
                step(ve.tensor_copy(gl[:, 0, 8:9], gy[:, TP - 1:TP]))
                step(ve.tensor_copy(gl[:, 2, 0:8], full[:, :, P // 2 - 1]))
                step(ve.tensor_copy(gl[:, 2, 8:9], gy[:, 8 * P + TAIL // 2 - 1:8 * P + TAIL // 2]))
                dve.wait_ge(sem("eg_ready"), i + 1)
                ve.tensor_tensor(gx[:, 0:8 * P].rearrange("p (c t) -> p c t", t=P), full,
                                 gl[:, 2, 0:8].unsqueeze(2).to_broadcast([P, 8, P]), ALU.subtract)\
                    .then_inc(sem("gd_ready"), 1)
                ve.tensor_scalar(gx[:, 8 * P:TP], gy[:, 8 * P:TP], gl[:, 2, 8:9], None, ALU.subtract)\
                    .then_inc(sem("gd_ready"), 1)
                ve.tensor_tensor(gl[:, 1, :], gl[:, 0, :], gl[:, 2, :], ALU.subtract).then_inc(sem("gl_ready"), 1)
                step(ve.memset(gx[:, TP:T], 1.0))
                step(ve.memset(gy[:, TP:T], 1.0))
                dve.wait_ge(sem("decays"), 3 * i + 3)
                for c, (c0, cw) in enumerate(CHUNKS):
                    filled(A3[c])
                    read(A3[c], ve.scalar_tensor_tensor(out=qe[:, c0:c0 + cw], in0=psum[:, A3[c], 0:cw],
                                                        scalar=GDK ** -0.5, in1=gx[:, c0:c0 + cw],
                                                        op0=ALU.mult, op1=ALU.mult))
                for c, (c0, cw) in enumerate(CHUNKS):
                    filled(B3[c])
                    read(B3[c], ve.tensor_tensor(ke[:, c0:c0 + cw], psum[:, B3[c], 0:cw], gy[:, c0:c0 + cw],
                                                 ALU.mult))
                skip(A3 + G_KTURN + B3 + G_VTURN[0] + A3 + G_VTURN[1] + B3)
                for c in range(NT):
                    n, par, b = width(c), c % 2, 2 * (c % 2)
                    filled(b)
                    if c >= 2:
                        dve.wait_ge(bank_full[4 + par], B.before(4 + par))
                    read(b, ve.tensor_tensor(gsc[0:n, par, :, 0:n],
                                             psum[0:n, b:b + 2, 0:n],
                                             tri[0:n, 0:n].unsqueeze(1).to_broadcast([n, 2, n]), ALU.mult))
                    filled(6 + par)
                    for h in range(2):
                        rows = slice(64 * h, 64 * h + 64)
                        ins = ve.tensor_scalar(kvs[rows, :], psum[rows, 6 + par, h * P:(h + 1) * P],
                                               gl[rows, 1, c:c + 1], None, ALU.mult)
                        if h == 1:
                            read(6 + par, ins)
                        else:
                            ins.then_inc(sem("kvs_half"), 1)
                    settled(6 + par)
                    dve.wait_ge(sem("kvs_half"), NT * i + c + 1)
                    if c == 0:
                        ins = ve.tensor_copy(stt[:, :], kvs[:, :])
                    else:
                        ins = ve.scalar_tensor_tensor(out=stt[:, :], in0=stt[:, :], scalar=gl[:, 0, c:c + 1],
                                                      in1=kvs[:, :], op0=ALU.mult, op1=ALU.add)
                    ins.then_inc(sem("state_ready"), 1)
                    dve.wait_ge(sem("state_ready"), NT * i + c + 1)
                    if c > 0:
                        skip([4 + (c - 1) % 2])
                    if c < NT - 1:
                        if c > 0:
                            dve.wait_ge(bank_full[4 + (c - 1) % 2], B.before(4 + (c - 1) % 2))
                        for h in range(2):
                            rows = slice(64 * h, 64 * h + 64)
                            ins = ve.tensor_scalar(stp[rows, (c + 1) % 2, h, :], stt[rows, :],
                                                   gl[rows, 2, c + 1:c + 2], None, ALU.mult)
                            if h == 1:
                                ins.then_inc(sem("stp_ready"), 1)
                            else:
                                ins.then_inc(sem("stp_half"), 1)
                skip([4 + (NT - 1) % 2])
                dve.wait_ge(sem("sst_loaded"), 32 * i + 32)
                dve.wait_ge(bank_full[4 + (NT - 1) % 2], B.before(4 + (NT - 1) % 2))
                for m in range(4):
                    b = G_VB[m]
                    filled(b)
                    if m > 0:
                        dve.wait_ge(sem("sst_ready"), NB * i + 2 * m)
                    for q in range(2):
                        n = 2 * m + q
                        for h in range(2):
                            rows = slice(64 * h, 64 * h + 64)
                            ins = ve.tensor_scalar(gsc[rows, q, 0, :],
                                                   psum[rows, b, 256 * q + P * h:256 * q + P * h + P],
                                                   ke[rows, TP + n:TP + n + 1], None, ALU.mult)
                            if q == 1 and h == 1:
                                read(b, ins)
                            else:
                                ins.then_inc(sem("outer"), 1)
                    settled(b)
                    dve.wait_ge(sem("outer"), 12 * i + 3 * m + 3)
                    for q in range(2):
                        n = 2 * m + q
                        ve.scalar_tensor_tensor(out=sst[:, n, :], in0=sst[:, n, :], scalar=eg[:, n:n + 1],
                                                in1=gsc[:, q, 0, :], op0=ALU.mult, op1=ALU.add)\
                            .then_inc(sem("sst_ready"), 1)
                skip([G_OS] + A3 + B3)
                for b in range(6):
                    settled(b)
                dve.wait_ge(sem("go_ready"), 10 * i + 10)
                step(ve.reciprocal(gsq[:, :, :], gsq[:, :, :]))
                step(ve.tensor_tensor(go[:, :, :], go[:, :, :], gsq[:, :, :], ALU.mult))
                for h in range(2):
                    g1 = gated[:, bass.ds(2 * i + h, 1), :]
                    ve.scalar_tensor_tensor(out=g1, in0=go[:, h:h + 1, :], scalar=gng[:, 0:1], in1=g1,
                                            op0=ALU.mult, op1=ALU.mult).then_inc(sem("gated_ready"), 1)
                dve.wait_ge(sem("gated_ready"), 2 * i + 2)
                dve.wait_ge(sem("stt_stored"), 32 * i + 32)
                dve.wait_ge(sem("sst_stored"), 32 * i + 32)
                while steps[0] < PER:
                    steps[0] += 1
                    ve.sem_inc(sem("gla_steps"), 1)
                B.end(2)
            for h in range(GH):
                dve.wait_ge(sem("og_high"), h + 1)
                ve.tensor_tensor(ol[:, 4 + h, :], gated[:, h, :], f(oh[:, 4 + h, :]), ALU.subtract)\
                    .then_inc(sem("o_split"), 1)

            with dve.Fori(0, KT) as m:
                B.loop(m, [2, 2, 2, 2, 2, 2, 0, 0])
                skip(A3 + B3)
                for c, (c0, cw) in enumerate(CHUNKS):
                    b = A3[c]
                    filled(b)
                    mx_ = mixed[:, bass.ds(m, 1), c0:c0 + cw]
                    read(b, ve.tensor_tensor(mx_, mx_, psum[:, b:b + 1, 0:cw], ALU.mult))
                for c, (c0, cw) in enumerate(CHUNKS):
                    b = B3[c]
                    filled(b)
                    s_ = sgb[:, c0:c0 + cw]
                    read(b, ve.tensor_tensor(s_, s_, psum[:, b, 0:cw], ALU.mult))
                    settled(A3[c])
                    settled(b)
                    mx_ = mixed[:, bass.ds(m, 1), c0:c0 + cw]
                    ve.tensor_tensor(mx_, mx_, sgb[:, c0:c0 + cw].unsqueeze(1), ALU.add)\
                        .then_inc(sem("mixed_ready"), 1)
                B.end(KT)
            for c, (c0, cw) in enumerate(CHUNKS):
                for q in range(2):
                    dve.wait_ge(sem("mixed_high"), 2 * c + q + 1)
                    four = slice(4 * q, 4 * q + 4)
                    ve.tensor_tensor(ol[:, four, c0:c0 + cw], mixed[:, four, c0:c0 + cw],
                                     f(oh[:, four, c0:c0 + cw]), ALU.subtract).then_inc(sem("mixed_split"), 1)
            dve.wait_ge(sem("mixed_split"), 6)
            n = 0
            for m in range(KT):
                for c, (c0, cw) in enumerate(CHUNKS):
                    b = (A3, B3)[m % 2][c]
                    cols = slice(c0, c0 + cw)
                    y = mixed[:, m, cols]
                    filled(b)
                    read(b, ve.scalar_tensor_tensor(out=y, in0=f(xh[:, m, cols]), scalar=ALPHA,
                                                    in1=psum[:, b, 0:cw], op0=ALU.mult, op1=ALU.add))
                    settled(b)
                    ve.scalar_tensor_tensor(out=y, in0=f(xl[:, m, cols]), scalar=ALPHA, in1=y,
                                            op0=ALU.mult, op1=ALU.add).then_inc(sem("residual"), 1)
                    n += 1
                    dve.wait_ge(sem("residual"), n)
                    if m == 0:
                        ins = ve.tensor_copy(ysum[:, cols], y)
                    else:
                        dve.wait_ge(sem("ysum_part"), n - 3)
                        ins = ve.tensor_tensor(ysum[:, cols], ysum[:, cols], y, ALU.add)
                    ins.then_inc(sem("ln1_sum") if m == KT - 1 else sem("ysum_part"), 1)

            def norm(tag, low_too):
                mean_full = []
                for b in MEAN_BANKS:
                    mean_full.append(B.after(b))
                    B.use(b)
                sq_free = []
                for b in SQ_BANKS:
                    B.use(b)
                    sq_free.append(B.before(b))

                def deviations(c):
                    c0, cw = CHUNKS[c]
                    b = MEAN_BANKS[c]
                    dve.wait_ge(bank_full[b], mean_full[c])
                    for q in range(2):
                        y = mixed[:, 4 * q:4 * q + 4, c0:c0 + cw]
                        ve.scalar_tensor_tensor(out=y, in0=psum[:, b, 0:cw].unsqueeze(1).to_broadcast([P, 4, cw]),
                                                scalar=-1.0 / D, in1=y, op0=ALU.mult, op1=ALU.add)\
                            .then_inc(sem(f"{tag}_dev"), 1)
                    dve.wait_ge(sem(f"{tag}_dev"), 2 * c + 2)
                    dve.sem_inc(bank_free[b], 1)

                def normalise(c):
                    c0, cw = CHUNKS[c]
                    dve.wait_ge(bank_free[SQ_BANKS[c]], sq_free[c])
                    r = yrst[:, c0:c0 + cw]
                    ve.reciprocal(r, r).then_inc(sem(f"{tag}_root"), 1)
                    dve.wait_ge(sem(f"{tag}_root"), c + 1)
                    for q in range(2):
                        y = mixed[:, 4 * q:4 * q + 4, c0:c0 + cw]
                        ve.tensor_tensor(y, y, r.unsqueeze(1).to_broadcast([P, 4, cw]), ALU.mult)\
                            .then_inc(sem(f"{tag}_norm"), 1)

                def lows(c):
                    if not low_too:
                        return
                    c0, cw = CHUNKS[c]
                    for q in range(2):
                        four = slice(4 * q, 4 * q + 4)
                        dve.wait_ge(sem("x1_high"), 2 * c + q + 1)
                        ve.tensor_tensor(xl[:, four, c0:c0 + cw], mixed[:, four, c0:c0 + cw],
                                         f(xh[:, four, c0:c0 + cw]), ALU.subtract).then_inc(sem("x1_split"), 1)
                deviations(0)
                deviations(1)
                normalise(0)
                deviations(2)
                normalise(1)
                lows(0)
                normalise(2)
                lows(1)
                lows(2)
            norm("ln1", True)
            dve.wait_ge(sem("y_scaled"), KT)

            with dve.Fori(0, FGROUPS) as g:
                B.loop(g, FFN_PER)
                for u in range(2):
                    skip(A3)
                    for c, (c0, cw) in enumerate(CHUNKS):
                        n, b = 3 * u + c, B3[c]
                        settled(A3[c])
                        filled(b)
                        ve.tensor_tensor(hf[:, n % 2, 0:cw], sg[:, u, c0:c0 + cw], psum[:, b, 0:cw], ALU.mult)\
                            .then_inc(sem("hidden"), 1)
                        B.use(b)
                        dve.wait_ge(sem("hidden_high"), 6 * g + n + 1)
                        ve.tensor_tensor(hl[:, u, c0:c0 + cw], hf[:, n % 2, 0:cw], f(hh[:, u, c0:c0 + cw]),
                                         ALU.subtract).then_inc(sem("hidden_split"), 1)
                        dve.sem_inc(bank_free[b], 1)
                for c, (c0, cw) in enumerate(CHUNKS):
                    for m in range(KT):
                        b = OUT_BANKS[m]
                        filled(b)
                        y = mixed[:, m, c0:c0 + cw]
                        read(b, ve.tensor_tensor(y, y, psum[:, b, 0:cw], ALU.add))
                for b in range(8):
                    settled(b)
                B.end(FGROUPS)
            for c, (c0, cw) in enumerate(CHUNKS):
                ve.tensor_reduce(ysum[:, c0:c0 + cw], mixed[:, :, c0:c0 + cw].rearrange("p k t -> p t k"), AX,
                                 ALU.add).then_inc(sem("ln2_sum"), 1)
            norm("ln2", False)
            for t in range(NT):
                w = P if t < 8 else NB
                b0, b1 = (2 * t) % 6, (2 * t + 1) % 6
                B.use(b0)
                filled(b1)
                if t >= 2:
                    dve.wait_ge(sem(f"y_stored{t % 2}"), 16 * (t // 2))
                read(b1, ve.tensor_copy(yout[0:w, t % 2, 512:1024], psum[0:w, b1, :]))


_OUTS = [("y_prompt", (1, SEQ, D)), ("y_sample", (NB, 1, D)),
         ("k_prompt", (1, 1, TP, FH, DH)), ("v_prompt", (1, 1, TP, FH, DH)), ("lf_prompt", (1, 1, TP, FH)),
         ("gla_prompt", (1, 1, GH, GDK, GDV)),
         ("k_sample", (1, NB, 1, FH, DH)), ("v_sample", (1, NB, 1, FH, DH)), ("lf_sample", (1, NB, 1, FH)),
         ("gla_sample", (1, NB, GH, GDK, GDV))]


def kernel(**inputs):
    import numpy as _np
    import concourse.bacc as _bacc
    from concourse.bass_utils import run_bass_kernel_spmd as _run

    nc = _bacc.Bacc("TRN2", target_bir_lowering=False, num_devices=1)
    arrays, ins, outs = {}, {}, {}
    for name in inputs:
        a = _np.ascontiguousarray(inputs[name])
        arrays[f"in_{name}"] = a
        ins[name] = nc.dram_tensor(f"in_{name}", a.shape, mybir.dt.from_np(a.dtype), kind="ExternalInput").ap()
    for name, shape in _OUTS:
        outs[name] = nc.dram_tensor(f"out_{name}", shape, F32, kind="ExternalOutput").ap()
    build(nc, ins, outs)
    r = _run(nc, [arrays], core_ids=[0])
    return tuple(r.results[0][f"out_{name}"] for name, _ in _OUTS)
```

```python
from contextlib import ExitStack

import numpy as np
import concourse.bass as bass
from concourse import mybir

F32 = mybir.dt.float32
F32R = mybir.dt.float32r
BF16 = mybir.dt.bfloat16
I32 = mybir.dt.int32
ALU = mybir.AluOpType
ACT = mybir.ActivationFunctionType
AX = mybir.AxisListType.X

P = 128
D = 1024
KT = D // P
META, SEQ, NB = 16, 1024, 8
TP = META + SEQ
T = TP + NB
NT = 9
TAIL = TP - 8 * P
CHUNKS = [(0, 352), (352, 352), (704, 344)]
FH, DH = 8, 64
FW = FH * DH
GH, GDK, GDV = 4, 64, 128
GK, GV = GH * GDK, GH * GDV
RANK = 16
TAU = 16.0
DFF = 2816
PAGE, NPAGE = 128, 8
NPOOL = 80
ALPHA = 2.0 ** 0.25
NEG = -1e30
O_FA = 3 * FW
O_QB = O_FA + FH
O_KB = O_QB + GK
O_VB = O_KB + GK
O_RB = O_VB + GV
O_AL = O_RB + GV
O_GA = O_AL + RANK
O_GB = O_GA + D

RING = 3
PAN_QKV = 1
PAN_GLA = PAN_QKV + 12
PAN_MERGE = PAN_GLA + 12
PAN_O = PAN_MERGE + 24
PAN_FFN = PAN_O + 8
FGROUPS = DFF // (2 * P)
PANELS = PAN_FFN + 6 * FGROUPS
ROW_ALR = 32


def width(t):
    return P if t < 8 else TAIL


SEG = 384
SEGS = -(-TP // SEG)
NI = 2 * NT
PER_SEG = SEG // P
GROUPS = 2 * SEGS


def probability_tiles():
    out = []
    for k in range(GROUPS):
        h, s = divmod(k, SEGS)
        q0, q1 = SEG * s, min(SEG * (s + 1), TP)
        n = -(-q1 // P)
        for t in range(n):
            c0 = max(q0, P * t)
            out.append((k, t, h, t, c0, q1 - c0, t == n - 1))
    return out


TILES = probability_tiles()
NTILE = len(TILES)
TILES_TO = [sum(x[0] <= k for x in TILES) for k in range(GROUPS)]
FIRST = [min(x for x in range(NTILE) if TILES[x][0] == k) for k in range(GROUPS)] + [NTILE]
ITEM_AT = {0: 6, 2: 7, 4: 8, 6: 9, 8: 10, 10: 11, 11: 12, 13: 13, 16: 14, 18: 15, 19: 16, 23: 17}
ROWS_AT = {1: 1, 7: 2, 15: 3, 18: 4, 25: 5}
OUT_AT = [x + 4 for x in FIRST[1:GROUPS]]
ST_BANKS, LAG, RING_P = [7, 3, 4], 2, 4


class Banks:

    def __init__(self):
        self.n, self.at, self.per = [0] * 8, None, [0] * 8

    def loop(self, register, per):
        self.base, self.at, self.per = list(self.n), register, per

    def end(self, times):
        assert [a - b for a, b in zip(self.n, self.base)] == self.per, (self.n, self.base, self.per)
        self.n = [b + times * p for b, p in zip(self.base, self.per)]
        self.at, self.per = None, [0] * 8

    def before(self, b):
        return self.n[b] + (self.at * self.per[b] if self.at is not None and self.per[b] else 0)

    def after(self, b):
        return self.n[b] + 1 + (self.at * self.per[b] if self.at is not None and self.per[b] else 0)

    def use(self, b):
        self.n[b] += 1


XT_BANKS = [(2 * t + g) % 8 for t in range(NT) for g in range(2)]
K_TURN, V_TURN = [6, 7, 5], [3, 4, 6]
PAIR_PER = [1, 1, 1, 3, 3, 3, 2, 1]
G_LG, G_KTURN, G_VTURN = [6, 7, 6], [6, 7, 6], [[7, 6, 7], [6, 7, 6]]
G_VB, G_OS = [6, 7, 6, 7], 6
FFN_PER = [5, 5, 5, 5, 5, 5, 3, 3]
MEAN_BANKS, SQ_BANKS = [6, 7, 6], [7, 6, 7]
A3, B3 = [0, 1, 2], [3, 4, 5]
OUT_BANKS = [6, 7, 0, 1, 2, 3, 4, 5]
GATE_BANKS = [[4, 5, 6], [7, 4, 5], [6, 7, 4], [5, 6, 7]]
GLA_COLUMNS = [O_RB + P * m for m in range(GH)] \
    + [c for i in range(2) for c in (O_QB + P * i, O_KB + P * i, O_VB + 2 * P * i, O_VB + 2 * P * i + P)]
SILU = ACT.Silu
KV_STORES = 6


def build(nc, IN, OUT):
    es = ExitStack()
    with es:
        sems = {}

        def sem(name):
            if name not in sems:
                sems[name] = es.enter_context(nc.semaphore(name))
            return sems[name]

        bank_full = [sem(f"bank_full{b}") for b in range(8)]
        bank_free = [sem(f"bank_free{b}") for b in range(8)]
        raw_loaded = [sem(f"raw_loaded{s}") for s in range(RING)]
        psum = es.enter_context(nc.psum_tensor("psum", [P, 8, 512], F32))

        top = [-(-nc.sbuf_base // 32) * 32]

        def size(shape, dt):
            n = int(np.prod(shape[1:])) * (2 if dt == BF16 else 4)
            return -(-n // 32) * 32

        def keep(name, shape, dt=F32):
            t = nc.alloc_sbuf_tensor_at(name, shape, dt, offset=top[0])
            top[0] += size(shape, dt)
            return t

        def region(offset, limit):
            at = [offset]

            def put(name, shape, dt=F32):
                t = nc.alloc_sbuf_tensor_at(name, shape, dt, offset=at[0])
                at[0] += size(shape, dt)
                assert at[0] <= offset + limit, (name, at[0] - offset, limit)
                return t
            return put

        raw = keep("raw", [P, RING, D])
        wh, wl = keep("wh", [P, RING, D], F32R), keep("wl", [P, RING, D], F32R)
        xh, xl = keep("xh", [P, KT, T], F32R), keep("xl", [P, KT, T], F32R)
        ident = keep("ident", [P, P])
        identr = keep("identr", [P, P], F32R)
        ones = keep("ones", [P, P])
        onesr = keep("onesr", [2, P], F32R)
        tri = keep("tri", [P, P])
        lnp = keep("lnp", [P, 4, KT])
        gng = keep("gng", [P, 1])
        bfc = keep("bfc", [FH, 1])
        bac = keep("bac", [P, 2])
        pages = keep("pages", [1, NB * NPAGE], I32)
        eps = keep("eps", [P, 2])
        OHB = top[0]
        oh = keep("oh", [P, 8, T], F32R)
        OLB = top[0]
        ol = keep("ol", [P, 8, T], F32R)
        R1 = top[0]
        R1N = (nc.sbuf_usable_end - R1) // 32 * 32
        HALF = 4 * T * 4
        EARLY, WA = size([P, P], F32) + 3 * size([P, P], BF16), size([RANK, GK], F32)
        e = region(R1 + R1N - EARLY - WA, EARLY + WA)
        low = e("low", [P, P])
        identb = e("identb", [P, P], BF16)
        later = e("later", [P, P], BF16)
        early = e("early", [P, P], BF16)
        wa2 = e("wa2", [RANK, GK])
        RE = R1 + R1N - EARLY - WA
        at_a = lambda: region(OHB + HALF, HALF)
        at_b = lambda: region(OLB + HALF, HALF)
        at_c = lambda: region(R1, RE - R1)

        xstage, xlast = at_c()("xstage", [P, 8, D]), at_a()("xlast", [TAIL + NB, D])
        a, b = at_a(), at_b()
        fz, fe, lfT = a("fz", [FH, T]), a("fe", [FH, T]), a("lfT", [FH, T])
        negc, lones = b("negc", [FH, TP]), b("lones", [FH, TP])
        a, b, c = at_a(), at_b(), at_c()
        alrT = c("alrT", [RANK, T])
        sq_tok, skv = c("sq_tok", [NB, FW]), c("skv", [32 + NB, FW])
        lfp = c("lfp", [P, NB, NPAGE, FH])
        svT = c("svT", [P, 4, NB])
        slf = c("slf", [NB, FH])
        LFP = R1 + size([P, T], F32) + 2 * size([NB, FW], F32)
        C_AFTER = LFP + size([P, NB, NPAGE, FH], F32) + size([P, 4, NB], F32) + size([NB, FH], F32)
        qh, ql, kh, kl = (a(x, [P, T], F32R) for x in ("qh", "ql", "kh", "kl"))
        cb, vh, vl = b("cb", [P, 2, TP]), b("vh", [P, T], F32R), b("vl", [P, T], F32R)
        vx, k_tok = c("vx", [P, NT, 3 * DH]), c("k_tok", [P, NT, P])
        pt, of = c("pt", [P, RING_P, SEG]), c("of", [P, 2, SEG])
        nmT = c("nmT", [2, 2, SEG], F32R)
        nmax, nms = c("nmax", [P, NI]), c("nms", [P, NI, 2], F32R)
        negc_tok, nck = c("negc_tok", [P, NT, FH]), c("nck", [P, NT, 2])
        lf_tok = c("lf_tok", [P, NT, FH])
        SMALL = 32 * 80
        LFS = R1 + R1N - WA - HALF - SMALL - 2048
        a, b, c = at_a(), at_b(), region(C_AFTER, LFS - C_AFTER)
        kv = [a("kv0", [P, NPAGE, FW]), b("kv1", [P, NPAGE, FW])]
        later_rows = c("later_rows", [P, P])
        ss = c("ss", [P, NB, NPAGE, FH])
        lfs = nc.alloc_sbuf_tensor_at("lfs", [P, NB, NPAGE, FH], F32, offset=LFS)
        rest = region(LFS + 2048, SMALL)
        sqk = nc.alloc_sbuf_tensor_at("sqk", [NB, FW], F32, offset=LFS)
        own_v = [nc.alloc_sbuf_tensor_at(f"own_v{x}", [FH, FW], F32, offset=o)
                 for x, o in enumerate([LFS, LFP])]
        dself, sbc, mbc = rest("dself", [NB, NB, FH]), rest("sbc", [P, NB, FH]), rest("mbc", [P, NB, FH])
        mx, mcol, dmx = rest("mx", [P, NB, FH]), rest("mcol", [64, 1]), rest("dmx", [64, 64])
        den, spr = rest("den", [P, NB, FH]), rest("spr", [P, NB, FH])
        sself = rest("sself", [NB, FH])
        onum = rest("onum", [P, 4, NB])
        gated = nc.alloc_sbuf_tensor_at("gated", [P, 4, T], F32, offset=R1 + R1N - WA - HALF)
        a, b, c = at_a(), at_b(), region(R1 + size([P, T], F32), R1N - WA - HALF - size([P, T], F32))
        qe, ke, go = a("qe", [P, T]), a("ke", [P, T]), a("go", [P, 2, T])
        gx, gy = b("gx", [P, T]), b("gy", [P, T])
        gsq = nc.alloc_sbuf_tensor_at("gsq", [P, 2, T], F32, offset=OLB + HALF)
        sst = b("sst", [P, NB, P])
        gsc = b("gsc", [P, 2, 2, P])
        stt, kvs, stp = b("stt", [P, P]), b("kvs", [P, P]), c("stp", [P, 2, 2, P])
        vb_tok, ke_tok = c("vb_tok", [P, NT, 2 * P]), c("ke_tok", [P, NT, P])
        gvT = nc.alloc_sbuf_tensor_at("gvT", [P, T], F32, offset=OHB + HALF + 2 * size([P, T], F32))
        gl, eg, vs_tok = c("gl", [P, 3, NT]), c("eg", [P, NB]), b("vs_tok", [NB, 2 * P])
        wai, bai = c("wai", [RANK, P]), c("bai", [P, 1])
        c = region(R1, R1N)
        mixed = c("mixed", [P, KT, T])
        sgb = c("sgb", [P, T])
        ysum = nc.alloc_sbuf_tensor_at("ysum", [P, T], F32, offset=R1 + KT * T * 4)
        z = region(OHB, 16 * T * 4)
        hh, hl = z("hh", [P, 2, T], F32R), z("hl", [P, 2, T], F32R)
        sg, hf = z("sg", [P, 2, T]), z("hf", [P, 2, 352])
        ysq, yrst = z("ysq", [P, 2, KT, 352]), z("yrst", [P, T])
        yout = z("yout", [P, 2, D])
        negc_dram = nc.dram_tensor("negc_scratch", [FH, TP], F32, kind="Internal").ap()

        def bank(b):
            return psum[:, b, :]

        def wt(buf, slot, k):
            return buf[:, slot, k * P:(k + 1) * P]

        def f(ap):
            return ap.bitcast(F32)

        def apart(engine):
            engine.sem_inc(sem(f"apart_{str(engine.engine).split('.')[-1]}"), 1)

        def fill(engine, n, parity):
            cache = IN["cache_k"][0] if n < NB else IN["cache_v"][0]
            if n >= 2:
                engine.wait_ge(sem("kv_used"), n - 1)
            for p in range(parity, NPAGE, 2):
                at = (n % NB) * NPAGE + p
                r = engine.value_load(pages[0:1, at:at + 1], min_val=0, max_val=NPOOL - 1)
                engine.dma_start(kv[n % 2][:, p, :],
                                 cache[bass.ds(r, 1), :, :, :].rearrange("a k h d -> (a k) (h d)"))\
                    .then_inc(sem(f"kv_loaded{n % 2}"), 16)

        w_in = IN["w_in"][0]
        block = es.enter_context(nc.Block())

        @block.sync
        def _(sp):
            def small(dst, src):
                sp.dma_start(dst, src, allow_slow_non_contiguous=True).then_inc(sem("params_loaded"), 16)

            def halves(slot, parts):
                for dst, src in parts:
                    sp.dma_start(dst, src).then_inc(raw_loaded[slot], 16)

            def columns(slot, w, col):
                src = w.rearrange("(k p) n -> p k n", p=P)
                dst = raw[:, slot, :].rearrange("p (k n) -> p k n", n=P)
                halves(slot, [(dst[:, 4 * m:4 * m + 4, :], src[:, 4 * m:4 * m + 4, bass.ds(col, P)])
                              for m in range(2)])

            def panel_free(p):
                if isinstance(p, int) and p < RING:
                    return
                sp.wait_ge(sem("panel_split"), p - RING + 1)
                if not isinstance(p, int):
                    apart(sp)

            for t in range(NT):
                rows = P if t < 8 else TAIL + NB
                if t == 0:
                    sp.dma_start(xstage[0:META, 0, :], IN["meta"]).then_inc(sem("x_loaded0"), 16)
                    sp.dma_start(xstage[META:P, 0, :], IN["x_prompt"][0, 0:P - META, :])\
                        .then_inc(sem("x_loaded0"), 16)
                elif t < 8:
                    sp.dma_start(xstage[:, t, :], IN["x_prompt"][0, P * t - META:P * t + P - META, :])\
                        .then_inc(sem(f"x_loaded{t}"), 16)
                else:
                    sp.dma_start(xlast[0:TAIL, :], IN["x_prompt"][0, SEQ - TAIL:SEQ, :])\
                        .then_inc(sem("x_loaded8"), 16)
                    sp.dma_start(xlast[TAIL:TAIL + NB, :], IN["x_sample"][:, 0, :])\
                        .then_inc(sem("x_loaded8"), 16)
            sp.wait_ge(sem("narrow_zeroed"), 1)
            src = w_in.rearrange("(k p) n -> p k n", p=P)
            dst = raw[:, 0, :].rearrange("p (k n) -> p k n", n=P)
            halves(0, [(dst[:, :, 0:FH], src[:, :, O_FA:O_FA + FH]),
                       (dst[:, :, ROW_ALR:ROW_ALR + RANK], src[:, :, O_AL:O_AL + RANK])])
            columns(1, w_in, 0)
            columns(2, w_in, FW)
            for m, name in enumerate(["ln1_g", "ln1_b", "ln2_g", "ln2_b"]):
                small(lnp[:, m, :], IN[name][0].rearrange("(k p) -> p k", p=P))
            small(gng[:, :], IN["gla_norm_g"][0].rearrange("(p a) -> p a", a=1))
            small(bfc[:, :], IN["b_f"][0].rearrange("(p a) -> p a", a=1))
            small(wa2[:, :], IN["w_a2"][0])
            small(bac[:, :], IN["b_a"][0].rearrange("(k p) -> p k", p=P))
            small(pages[:, :], IN["page_table"].rearrange("(a b) p -> a (b p)", a=1))
            panel_free(3)
            columns(0, w_in, 2 * FW)

            def spread(j):
                sp.dma_start(cb[:, :, :], negc_dram[bass.ds(2 * j, 2), :].partition_broadcast(P))\
                    .then_inc(sem("cb_loaded"), 16)
            sp.wait_ge(sem("negc_ready"), 1)
            sp.dma_start(negc_dram, negc[:, :]).then_inc(sem("negc_stored"), 16)
            sp.wait_ge(sem("negc_stored"), 16)
            sp.wait_ge(sem("negc_turned"), 1)
            spread(0)

            def page(n, p):
                at = n * NPAGE + p
                return sp.value_load(pages[0:1, at:at + 1], min_val=0, max_val=NPOOL - 1)
            sp.wait_ge(sem("params_loaded"), 16 * 9)
            for n in range(NB):
                for p in range(NPAGE):
                    sp.dma_start(lfp[:, n, p, :],
                                 IN["cache_lf"][0][bass.ds(page(n, p), 1), :, :].rearrange("a k h -> (a k) h"))\
                        .then_inc(sem("lf_loaded"), 16)

            def store_pair(j):
                sp.wait_ge(sem("tok_ready"), j + 1)
                apart(sp)
                o = OUT["k_prompt"][0, 0].rearrange("t h d -> t (h d)")
                sp.dma_start(o[0:8 * P, bass.ds(P * j, P)].rearrange("(t p) c -> p t c", p=P),
                             k_tok[:, 0:8, :]).then_inc(sem("kv_stored"), 16)
                sp.dma_start(o[8 * P:TP, bass.ds(P * j, P)], k_tok[0:TAIL, 8, :])\
                    .then_inc(sem("kv_stored"), 16)
                o = OUT["v_prompt"][0, 0].rearrange("t h d -> t (h d)")
                for h in range(2):
                    sp.dma_start(o[0:8 * P, bass.ds(P * j + DH * h, DH)].rearrange("(t p) c -> p t c", p=P),
                                 vx[:, 0:8, 2 * DH * h:2 * DH * h + DH]).then_inc(sem("kv_stored"), 16)
                    sp.dma_start(o[8 * P:TP, bass.ds(P * j + DH * h, DH)],
                                 vx[0:TAIL, 8, 2 * DH * h:2 * DH * h + DH]).then_inc(sem("kv_stored"), 16)
            with sp.Fori(1, 4) as j:
                for m in range(3):
                    panel_free(PAN_QKV + 3 * j + m)
                    columns((1 + m) % RING, w_in, FW * m + P * j)
                store_pair(j - 1)
                sp.wait_ge(sem("scores_read"), NI * j)
                apart(sp)
                spread(j)

            store_pair(3)
            for m in range(5):
                panel_free(PAN_GLA + m)
                columns((PAN_GLA + m) % RING, w_in, GLA_COLUMNS[m])
            sp.wait_ge(sem("o_done"), 1)
            sp.wait_ge(sem("kv_stored"), KV_STORES * 16 * 4)
            def gla_panel(m):
                panel_free(PAN_GLA + m)
                columns((PAN_GLA + m) % RING, w_in, GLA_COLUMNS[m])
            for n in range(2 * NB):
                fill(sp, n, 0)
                if n in (1, 3, 5):
                    gla_panel(5 + n // 2)

            def state_load(i):
                for hh_ in range(2):
                    sp.dma_start(sst[64 * hh_:64 * hh_ + 64, :, :],
                                 IN["state_gla"][0][:, bass.ds(2 * i + hh_, 1), :, :]
                                 .rearrange("b h d v -> d (b h) v")).then_inc(sem("sst_loaded"), 16)
            sp.wait_ge(sem("samples_done"), 1)
            state_load(0)
            for m in range(8, len(GLA_COLUMNS)):
                gla_panel(m)
            sp.wait_ge(sem("sst_stored"), 32)
            state_load(1)

            def merge_panels(m):
                panel_free(PAN_MERGE + 3 * m)
                columns(1, w_in, O_GA + P * m)
                panel_free(PAN_MERGE + 3 * m + 1)
                columns(2, w_in, O_GB + P * m)
                panel_free(PAN_MERGE + 3 * m + 2)
                dst = raw[:, 0, :].rearrange("p (k n) -> p k n", n=P)
                halves(0, [(dst[:, 4 * g:4 * g + 4, :],
                            IN[name][0].rearrange("(k p) n -> p k n", p=P)[:, :, bass.ds(P * m, P)])
                           for g, name in enumerate(["w_pa", "w_pb"])])
            with sp.Fori(0, KT) as m:
                merge_panels(m)
            for m in range(8):
                panel_free(PAN_O + m)
                columns((PAN_O + m) % RING, IN["w_o"][0], P * m)
            with sp.Fori(0, FGROUPS) as g:
                for m in range(4):
                    panel_free(PAN_FFN + 6 * g + m)
                    columns(m % RING, IN["w_up" if m % 2 else "w_gate"][0], 2 * P * g + P * (m // 2))
                for m in range(2):
                    panel_free(PAN_FFN + 6 * g + 4 + m)
                    slot = (4 + m) % RING
                    dst = raw[:, slot, :].rearrange("p (k n) -> p k n", k=2)
                    src = IN["w_down"][0][bass.ds(2 * P * g, 2 * P), :].rearrange("(k p) n -> p k n", p=P)
                    halves(slot, [(dst[:, k, :], src[:, k, 512 * m:512 * m + 512]) for k in range(2)])

        @block.gpsimd
        def _(pool):
            pool.memset(raw[:, 0, :], 0.0).then_inc(sem("narrow_zeroed"), 1)
            made = sem("made")
            pool.memset(ident[:, :], 0.0).then_inc(made, 1)
            pool.memset(ones[:, :], 1.0).then_inc(made, 1)
            pool.memset(later[:, :], 0.0).then_inc(made, 1)
            pool.wait_ge(made, 3)
            pool.affine_select(out=ident[:, :], in_=ident[:, :], compare_op=ALU.not_equal, fill=1.0, base=0,
                               pattern=[[-1, P]], channel_multiplier=1).then_inc(sem("ident_ready"), 1)
            pool.wait_ge(sem("ident_ready"), 1)
            pool.affine_select(out=tri[:, :], in_=ones[:, :], compare_op=ALU.is_ge, fill=0.0, base=0,
                               pattern=[[1, P]], channel_multiplier=-1).then_inc(made, 1)
            pool.wait_ge(made, 4)
            pool.affine_select(out=low[:, :], in_=ones[:, :], compare_op=ALU.is_gt, fill=0.0, base=0,
                               pattern=[[-1, P]], channel_multiplier=1).then_inc(made, 1)
            pool.wait_ge(made, 5)
            pool.tensor_copy(identb[:, :], ident[:, :]).then_inc(made, 1)
            pool.wait_ge(made, 6)
            pool.tensor_copy(early[:, :], later[:, :]).then_inc(made, 1)
            pool.wait_ge(made, 7)
            pool.affine_select(out=later[:, :], in_=later[:, :], compare_op=ALU.is_ge, fill=NEG, base=0,
                               pattern=[[-1, P]], channel_multiplier=1).then_inc(made, 1)
            pool.wait_ge(made, 8)
            pool.affine_select(out=early[:, :], in_=early[:, :], compare_op=ALU.is_ge, fill=NEG, base=0,
                               pattern=[[1, P]], channel_multiplier=-1).then_inc(made, 1)
            pool.wait_ge(made, 9)
            pool.tensor_copy(identr[:, :], ident[:, :]).then_inc(made, 1)
            pool.wait_ge(made, 10)
            pool.tensor_copy(onesr[:, :], ones[0:2, :]).then_inc(made, 1)
            pool.wait_ge(made, 11)
            pool.memset(eps[:, 0:1], 1e-6).then_inc(made, 1)
            pool.memset(eps[:, 1:2], 1e-5).then_inc(sem("consts_ready"), 1)

            def split(s, use, p):
                pool.wait_ge(raw_loaded[s], 32 * use)
                if not (isinstance(p, int) and p < RING):
                    pool.wait_ge(sem("panel_used"), p - RING + 1)
                apart(pool)
                pool.tensor_copy(wh[:, s, :], raw[:, s, :]).then_inc(sem("panel_high"), 1)
                pool.wait_ge(sem("panel_high"), p + 1)
                pool.tensor_tensor(wl[:, s, :], raw[:, s, :], f(wh[:, s, :]), ALU.subtract)\
                    .then_inc(sem("panel_split"), 1)
            for s in range(RING):
                split(s, 1, s)
            with pool.Fori(1, PANELS // RING) as i:
                for s in range(RING):
                    split(s, i + 1, RING * i + s)

        @block.tensor
        def _(pe):
            B = Banks()
            mm = nc.tensor.matmul

            def take(b):
                if isinstance(B.before(b), int) and B.before(b) == 0:
                    return
                pe.wait_ge(bank_free[b], B.before(b))

            def give(b, ins):
                ins.then_inc(bank_full[b], 1)
                B.use(b)

            def settled(b):
                pe.wait_ge(bank_free[b], B.before(b))

            def job(p, slot, banks, ks, xs, release=True, before_chunk=None, half=None, after=None):
                if p is not None:
                    pe.wait_ge(sem("panel_split"), p + 1)
                for c, (c0, cw) in enumerate(CHUNKS):
                    b = banks[c]
                    take(b)
                    if before_chunk is not None:
                        before_chunk(c)
                    out = psum[:, b, 0:cw]
                    for n, k in enumerate(ks):
                        w = (wt(wh, slot, k), wt(wl, slot, k))
                        x = [h[:, xs[1][n], c0:c0 + cw] for h in xs[0]]
                        first = mm(out, w[0], x[0], start=(n == 0), stop=False)
                        if release and c == 0 and n == 0:
                            first.then_inc(sem("panel_used"), 1)
                        mm(out, w[0], x[1], start=False, stop=False)
                        last = mm(out, w[1], x[0], start=False, stop=(n == len(ks) - 1))
                        if half is not None and n == 3:
                            half(c)
                    give(b, last)
                    if after is not None:
                        after(c)

            X8 = ((xh, xl), list(range(8)))
            ALL8 = list(range(8))

            pe.wait_ge(sem("ident_ready"), 1)
            for t in range(NT):
                rows = P if t < 8 else TAIL + NB
                pe.wait_ge(sem(f"x_loaded{t}"), 32 if t in (0, 8) else 16)
                src = xstage[0:rows, t, :] if t < 8 else xlast[:, :]
                for g in range(2):
                    b = XT_BANKS[2 * t + g]
                    take(b)
                    for k in range(4):
                        last = nc.tensor.transpose(psum[:, b, k * P:k * P + rows],
                                                   src[:, (4 * g + k) * P:(4 * g + k + 1) * P],
                                                   ident[0:rows, 0:rows])
                    give(b, last)
            pe.wait_ge(sem("consts_ready"), 1)

            for b in range(8):
                settled(b)
            job(0, 0, A3, ALL8, X8, release=False)
            take(3)
            pe.wait_ge(sem("lf_ready"), 1)
            for t in range(NT):
                w = width(t)
                nc.tensor.transpose(psum[0:w, 3, t * FH:(t + 1) * FH], lfT[:, t * P:t * P + w],
                                    ident[0:FH, 0:FH])
            last = nc.tensor.transpose(psum[0:NB, 3, NT * FH:(NT + 1) * FH], lfT[:, TP:T], ident[0:FH, 0:FH])
            give(3, last)
            take(4)
            pe.wait_ge(sem("negc_ready"), 1)
            for t in range(NT):
                w = width(t)
                last = nc.tensor.transpose(psum[0:w, 4, t * FH:(t + 1) * FH], negc[:, t * P:t * P + w],
                                           ident[0:FH, 0:FH])
            give(4, last)

            def turn(parts, banks, extra):
                def one(out, src, cols):
                    if len(src) == 1:
                        return nc.tensor.transpose(out, src[0][:, cols], ident[:, :])
                    mm(out, src[0][:, cols], identr[:, :], start=True, stop=False)
                    return mm(out, src[1][:, cols], identr[:, :], start=False, stop=True)
                for g, b in enumerate(banks):
                    take(b)
                    for t in range(4 * g, min(4 * g + 4, NT)):
                        w = width(t)
                        last = one(psum[0:w, b, (t - 4 * g) * P:(t - 4 * g + 1) * P], parts,
                                   slice(t * P, t * P + w))
                    if g == 2:
                        for m, e in enumerate(extra):
                            last = one(psum[0:NB, b, (m + 1) * P:(m + 2) * P], e, slice(TP, T))
                    give(b, last)

            with pe.Fori(0, 4) as j:
                B.loop(j, PAIR_PER)
                p = PAN_QKV + 3 * j

                def scores(n, at=0):
                    h, i = divmod(n, NT)
                    nq, nk = width(i), min(P * (i + 1), TP)
                    rows = slice(DH * h, DH * h + DH)
                    if n > 0:
                        pe.wait_ge(sem("scores_read"), NI * j + n)
                    if nk > 2 * 512:
                        pe.wait_ge(sem("rows_ready"), GROUPS * j + sum(x <= at for x in ROWS_AT) + 1)
                    if nq < P:
                        apart(pe)
                    for c0 in range(0, nk, 512):
                        c1 = min(c0 + 512, nk)
                        last = mm(psum[0:nq, c0 // 512, 0:c1 - c0], qh[rows, i * P:i * P + nq],
                                  kh[rows, c0:c1], start=True, stop=(c1 != nk))
                    d0 = i * P - c0
                    last = mm(psum[0:nq, c0 // 512, d0:d0 + nq], identb[0:nq, 0:nq], later[0:nq, 0:nq],
                              start=False, stop=True)
                    last.then_inc(sem("scores_full"), 1)

                def rows_of(k):
                    if k > 0:
                        pe.wait_ge(sem("rows_ready"), GROUPS * j + k)
                    pe.wait_ge(sem("max_split"), GROUPS * j + k + 1)
                    for q in range(PER_SEG):
                        n = PER_SEG * k + q
                        nq = width(n % NT)
                        if nq < P:
                            apart(pe)
                        last = mm(psum[0:2, 2, q * P:q * P + nq], nms[0:nq, n, :], identr[0:nq, 0:nq],
                                  start=True, stop=True)
                    last.then_inc(sem("rows_full"), 1)

                def tile_scores(x):
                    k, l, h, t, c0, n, _ = TILES[x]
                    rows, w, b = slice(DH * h, DH * h + DH), width(t), ST_BANKS[x % 3]
                    if x >= 3:
                        pe.wait_ge(sem("probs_ready"), NTILE * j + x - 2)
                    else:
                        settled(b)
                    if l == 0:
                        pe.wait_ge(sem("rows_ready"), GROUPS * j + k + 1)
                    if w < P:
                        apart(pe)
                    out, off = psum[0:w, b, 0:n], c0 % SEG
                    keys, queries = slice(P * t, P * t + w), slice(c0, c0 + n)
                    mm(out, kh[rows, keys], qh[rows, queries], start=True, stop=False)
                    mm(out, kh[rows, keys], ql[rows, queries], start=False, stop=False)
                    mm(out, kl[rows, keys], qh[rows, queries], start=False, stop=False)
                    diagonal = c0 == P * t
                    last = mm(out, onesr[:, 0:w], nmT[:, k % 2, off:off + n], start=False, stop=not diagonal)
                    if diagonal:
                        m = min(P, n)
                        last = mm(psum[0:w, b, 0:m], identb[0:w, 0:w], early[0:w, 0:m], start=False,
                                  stop=True)
                    last.then_inc(sem("tile_full"), 1)

                def mix(x):
                    k, l, h, t, c0, n, end = TILES[x]
                    w, b, off = width(t), 5 + k % 2, c0 % SEG
                    if l == 0 and k >= 2:
                        pe.wait_ge(sem("o_read"), GROUPS * j + k)
                    if x == 0:
                        for q in (3, 4, 5, 6):
                            settled(q)
                    pe.wait_ge(sem("probs_ready"), NTILE * j + x + 1)
                    if w < P:
                        apart(pe)
                    last = mm(psum[:, b, off:off + n], vx[0:w, t, DH * h:DH * h + P], pt[0:w, x % RING_P, 0:n],
                              start=(t == 0), stop=end)
                    last.then_inc(sem("mixed_in"), 1)

                job(p, 1, A3, ALL8, X8)
                pe.wait_ge(sem("o_read"), GROUPS * j + 1)
                job(p + 1, 2, B3, ALL8, X8)

                def first_scores(c):
                    if c == 0:
                        for b in A3:
                            settled(b)
                        pe.wait_ge(bank_free[4], B.before(4))
                        pe.wait_ge(bank_free[3], B.before(3))
                    if c == 1:
                        pe.wait_ge(bank_free[5], B.before(5))
                    scores(2 * c)
                job(p + 2, 0, B3, ALL8, X8, half=first_scores, after=lambda c: scores(2 * c + 1))
                values_read = [(b, B.before(b)) for b in B3]
                turn((kh, kl), K_TURN, [(kh, kl), (qh, ql)])
                rows_of(0)
                for b, uses in values_read:
                    pe.wait_ge(bank_free[b], uses)
                turn((vh, vl), V_TURN, [(vh, vl)])
                for x in range(NTILE):
                    tile_scores(x)
                    if x in ITEM_AT:
                        scores(ITEM_AT[x], x)
                    if x in ROWS_AT:
                        rows_of(ROWS_AT[x])
                    if x >= LAG:
                        mix(x - LAG)
                for x in range(NTILE - LAG, NTILE):
                    mix(x)
                pe.wait_ge(sem("scores_read"), NI * (j + 1))
                B.end(4)
            pe.wait_ge(sem("o_read"), 4 * GROUPS + 1)

            def spread_query(n):
                b = n % 2
                take(b)
                last = mm(bank(b), ident[0:NB, n:n + 1].to_broadcast([NB, P]), sq_tok[:, :], start=True,
                          stop=True)
                give(b, last)
            for b in range(8):
                settled(b)
            spread_query(0)
            spread_query(1)
            take(2)
            pe.wait_ge(sem("dself_ready"), 1)
            last = mm(psum[:, 2, 0:64], ones[0:NB, :], dself[:, :, :].rearrange("a b h -> a (b h)"),
                      start=True, stop=True)
            give(2, last)
            take(3)
            pe.wait_ge(sem("dself_ready"), 2)
            pe.wait_ge(sem("lfs_ready"), 1)
            pe.wait_ge(sem("lf_loaded"), 16 * NB * NPAGE)
            flat = lambda t: t[:, :, :, :].rearrange("q b p h -> q (b p h)")
            mm(bank(3), ones[:, :], flat(lfs), start=True, stop=False)
            mm(bank(3), later_rows[:, :], flat(lfp), start=False, stop=False)
            last = mm(psum[:, 3, :].rearrange("q (b p h) -> q b p h", b=NB, p=NPAGE), ones[0:NB, :],
                      dself[:, :, :].unsqueeze(2).to_broadcast([NB, NB, NPAGE, FH]), start=False, stop=True)
            give(3, last)
            for m in range(GH):
                job(PAN_GLA + m, (PAN_GLA + m) % RING, GATE_BANKS[m], ALL8, X8, before_chunk=lambda c:
                    spread_query(2 + (3 * m + c) // 2) if (3 * m + c) % 2 else None)
            take(4)
            pe.wait_ge(sem("mx_ready"), 1)
            last = nc.tensor.transpose(psum[0:64, 4, 0:P], mx[:, :, :].rearrange("q b h -> q (b h)"), ident[:, :])
            give(4, last)
            take(5)
            pe.wait_ge(sem("dmx_ready"), 1)
            last = mm(psum[:, 5, 0:64], ones[0:64, :], dmx[:, :], start=True, stop=True)
            give(5, last)
            take(6)
            pe.wait_ge(sem("sprobs_ready"), 2)
            last = mm(bank(6), ones[:, :], flat(ss), start=True, stop=True)
            give(6, last)
            take(7)

            def sample_values(n):
                f_, b = NB + n, n % 2
                pe.wait_ge(sem(f"kv_loaded{f_ % 2}"), 16 * NPAGE * (f_ // 2 + 1))
                take(b)
                for p in range(NPAGE):
                    last = mm(psum[0:FH, b, :], ss[:, n, p, :], kv[f_ % 2][:, p, :], start=(p == 0),
                              stop=(p == NPAGE - 1))
                give(b, last)

            def sample_outputs(n):
                settled(n % 2)
                for m in range(4):
                    last = mm(psum[:, 7, m * NB + n:m * NB + n + 1], own_v[n % 2][:, m * P:(m + 1) * P],
                              ones[0:FH, 0:1], start=True, stop=True)
                return last
            for n in range(NB):
                sample_values(n)
                if n > 0:
                    sample_outputs(n - 1)
            give(7, sample_outputs(NB - 1))

            for i in range(2):
                p = PAN_GLA + GH + 4 * i

                def gate_logits():
                    pe.wait_ge(sem("wai_ready"), 2 * i + 2)
                    for c, (c0, cw) in enumerate(CHUNKS):
                        take(G_LG[c])
                        last = mm(psum[:, G_LG[c], 0:cw], wai[:, :], alrT[:, c0:c0 + cw], start=True, stop=True)
                        give(G_LG[c], last)
                if i == 0:
                    gate_logits()
                job(p, p % RING, A3, ALL8, X8)
                if i == 1:
                    gate_logits()
                job(p + 1, (p + 1) % RING, B3, ALL8, X8)
                job(p + 2, (p + 2) % RING, A3, ALL8, X8)
                for b in B3:
                    settled(b)
                turn((ke,), G_KTURN, [])
                job(p + 3, (p + 3) % RING, B3, ALL8, X8)
                for b in A3:
                    settled(b)
                turn((gvT,), G_VTURN[0], [(gvT,)])
                for b in B3:
                    settled(b)
                turn((gvT,), G_VTURN[1], [(gvT,)])
                for b in range(8):
                    settled(b)

                for m in range(4):
                    b = G_VB[m]
                    take(b)
                    for q in range(2):
                        n = 2 * m + q
                        last = mm(psum[:, b, q * 256:(q + 1) * 256], ident[0:NB, n:n + 1].to_broadcast([NB, P]),
                                  vs_tok[:, :], start=True, stop=True)
                    give(b, last)
                def within(c):
                    n, b = width(c), 2 * (c % 2)
                    cols = slice(c * P, c * P + n)
                    take(b)
                    if n < P:
                        apart(pe)
                    for h in range(2):
                        rows = slice(64 * h, 64 * h + 64)
                        last = mm(psum[0:n, b + h, 0:n], ke[rows, cols], qe[rows, cols],
                                  start=True, stop=True)
                    give(b, last)
                    kvb = 6 + c % 2
                    take(kvb)
                    last = mm(psum[:, kvb, 0:2 * P], ke_tok[0:n, c, :], vb_tok[0:n, c, :], start=True, stop=True)
                    give(kvb, last)

                def outputs(c):
                    n, b = width(c), 4 + c % 2
                    take(b)
                    settled(2 * (c % 2))
                    if c > 0:
                        pe.wait_ge(sem("stp_ready"), 8 * i + c)
                    for h in range(2):
                        o = psum[:, b, h * P:h * P + n]
                        last = mm(o, vb_tok[0:n, c, h * P:(h + 1) * P], gsc[0:n, c % 2, h, 0:n], start=True,
                                  stop=(c == 0))
                        if c > 0:
                            last = mm(o, stp[:, c % 2, h, :], qe[:, c * P:c * P + n], start=False, stop=True)
                    give(b, last)
                for c in range(NT + 1):
                    if c < NT:
                        within(c)
                    if c > 0:
                        outputs(c - 1)
                take(6)
                take(7)
                pe.wait_ge(sem("sst_ready"), NB * (i + 1))
                for h in range(2):
                    rows = slice(64 * h, 64 * h + 64)
                    for n in range(NB):
                        last = mm(psum[:, G_OS + h, n:n + 1], sst[rows, n, :],
                                  qe[rows, TP + n:TP + n + 1], start=True, stop=True)
                give(G_OS, last)
                for h in range(2):
                    for c, (c0, cw) in enumerate(CHUNKS):
                        b = (A3, B3)[h][c]
                        take(b)
                        if h == 0 and c == 0:
                            for q in (0, 2, 4, 5, 6):
                                settled(q)
                        last = mm(psum[:, b, 0:cw], ones[:, :], gsq[:, h, c0:c0 + cw], start=True, stop=True)
                        give(b, last)

            with pe.Fori(0, KT) as m:
                B.loop(m, [2, 2, 2, 2, 2, 2, 0, 0])
                p = PAN_MERGE + 3 * m
                job(p, 1, A3, ALL8, X8)
                job(p + 1, 2, B3, ALL8, X8)
                pe.wait_ge(sem("o_split"), 4)
                job(p + 2, 0, A3, [0, 1, 2, 3], ((oh, ol), [0, 1, 2, 3]))
                job(None, 0, B3, [4, 5, 6, 7], ((oh, ol), [4, 5, 6, 7]), release=False)
                B.end(KT)

            for m in range(KT):
                job(PAN_O + m, (PAN_O + m) % RING, (A3, B3)[m % 2], ALL8, ((oh, ol), ALL8),
                    before_chunk=(lambda c: pe.wait_ge(sem("mixed_split"), 2 * c + 1)) if m == 0 else None,
                    half=(lambda c: pe.wait_ge(sem("mixed_split"), 2 * c + 2)) if m == 0 else None)

            def norm_sums(tag):
                for c, (c0, cw) in enumerate(CHUNKS):
                    b = MEAN_BANKS[c]
                    take(b)
                    pe.wait_ge(sem(f"{tag}_sum"), c + 1)
                    last = mm(psum[:, b, 0:cw], ones[:, :], ysum[:, c0:c0 + cw], start=True, stop=True)
                    give(b, last)
                for c, (c0, cw) in enumerate(CHUNKS):
                    b = SQ_BANKS[c]
                    take(b)
                    for k in range(KT):
                        pe.wait_ge(sem(f"{tag}_sq"), 2 * c + k // 4 + 1)
                        last = mm(psum[:, b, 0:cw], ones[:, :], ysq[:, c % 2, k, 0:cw], start=(k == 0),
                                  stop=(k == KT - 1))
                    give(b, last)
            norm_sums("ln1")

            with pe.Fori(0, FGROUPS) as g:
                B.loop(g, FFN_PER)
                p = PAN_FFN + 6 * g
                job(p, 0, A3, ALL8, X8, before_chunk=lambda c: pe.wait_ge(sem("x1_split"), 2 * c + 1),
                    half=lambda c: pe.wait_ge(sem("x1_split"), 2 * c + 2))
                job(p + 1, 1, B3, ALL8, X8)
                job(p + 2, 2, A3, ALL8, X8)
                job(p + 3, 0, B3, ALL8, X8)
                pe.wait_ge(sem("panel_split"), p + 5)
                pe.wait_ge(sem("panel_split"), p + 6)
                for c, (c0, cw) in enumerate(CHUNKS):
                    pe.wait_ge(sem("hidden_split"), 6 * g + 4 + c)
                    for m in range(KT):
                        b = OUT_BANKS[m]
                        take(b)
                        slot = (4 + m // 4) % RING
                        for k in range(2):
                            w = tuple(x[:, slot, k * 512 + (m % 4) * P:k * 512 + (m % 4 + 1) * P] for x in (wh, wl))
                            x = [x[:, k, c0:c0 + cw] for x in (hh, hl)]
                            out = psum[:, b, 0:cw]
                            first = mm(out, w[0], x[0], start=(k == 0), stop=False)
                            if (c, m, k) in ((0, 0, 0), (2, 4, 0)):
                                first.then_inc(sem("panel_used"), 1)
                            mm(out, w[0], x[1], start=False, stop=False)
                            last = mm(out, w[1], x[0], start=False, stop=(k == 1))
                        give(b, last)
                B.end(FGROUPS)

            norm_sums("ln2")
            for t in range(NT):
                c0, w = (META + t * P, P) if t < 8 else (TP, NB)
                pe.wait_ge(sem("ln2_aff"), KT * (1 if c0 + w <= 352 else 2 if c0 + w <= 704 else 3))
                for g in range(2):
                    b = (2 * t + g) % 6
                    take(b)
                    for k in range(4):
                        last = nc.tensor.transpose(psum[0:w, b, k * P:(k + 1) * P],
                                                   mixed[:, 4 * g + k, c0:c0 + w], ident[:, :])
                    give(b, last)


        @block.scalar
        def _(act):
            B = Banks()
            do = nc.scalar.activation

            def filled(b):
                act.wait_ge(bank_full[b], B.after(b))

            def read(b, ins):
                ins.then_inc(bank_free[b], 1)
                B.use(b)

            def settled(b):
                act.wait_ge(bank_free[b], B.before(b))

            def skip(banks):
                for b in banks:
                    B.use(b)

            for n in range(2 * NT):
                t, g, b = n // 2, n % 2, XT_BANKS[n]
                rows = P if t < 8 else TAIL + NB
                filled(b)
                src = bank(b).rearrange("p (k c) -> p k c", k=4)[:, :, 0:rows]
                do(xh[:, 4 * g:4 * g + 4, t * P:t * P + rows], src, ACT.Copy).then_inc(sem("xh_ready"), 1)
                skip([b])
            act.wait_ge(sem("params_loaded"), 16 * 9)
            act.wait_ge(sem("consts_ready"), 1)
            for c, (c0, cw) in enumerate(CHUNKS):
                filled(c)
                do(fz[:, c0:c0 + cw], psum[0:FH, c, 0:cw], ACT.Identity, bias=bfc[:, 0:1])\
                    .then_inc(sem("fz_ready"), 1)
                read(c, do(alrT[:, c0:c0 + cw], psum[ROW_ALR:ROW_ALR + RANK, c, 0:cw], ACT.Copy))
            act.wait_ge(sem("fz_ready"), 3)
            do(fe[:, :], fz[:, :], ACT.Abs).then_inc(sem("fe"), 1)
            act.wait_ge(sem("fe"), 1)
            do(fe[:, :], fe[:, :], ACT.Exp, scale=-1.0).then_inc(sem("fe"), 1)
            act.wait_ge(sem("fe"), 2)
            do(fe[:, :], fe[:, :], ACT.Ln, bias=1.0).then_inc(sem("fe"), 1)
            skip([3, 4])
            settled(3)
            act.wait_ge(sem("slf_ready"), 1)
            lf_out = OUT["lf_prompt"][0, 0]
            act.dma_start(lf_out[0:8 * P, :].rearrange("(t p) h -> p t h", p=P), lf_tok[:, 0:8, :])\
                .then_inc(sem("lf_stored"), 16)
            act.dma_start(lf_out[8 * P:TP, :], lf_tok[0:TAIL, 8, :]).then_inc(sem("lf_stored"), 16)
            act.dma_start(OUT["lf_sample"][0, :, 0, :], slf[:, :]).then_inc(sem("lf_stored"), 16)

            with act.Fori(0, 4) as j:
                B.loop(j, PAIR_PER)
                def high_halves(dst, banks, scale, also=None):
                    for c, (c0, cw) in enumerate(CHUNKS):
                        filled(banks[c])
                        if c == 2 and also is not None:
                            also(banks[c])
                        do(dst[:, c0:c0 + cw], psum[:, banks[c], 0:cw], ACT.Copy, scale=scale)\
                            .then_inc(sem("qkv_high"), 1)
                        B.use(banks[c])
                def row_copy(k):
                    act.wait_ge(sem("rows_full"), GROUPS * j + k + 1)
                    n = min(SEG, TP - SEG * (k % SEGS))
                    do(nmT[:, k % 2, 0:n], psum[0:2, 2, 0:n], ACT.Copy).then_inc(sem("rows_ready"), 1)

                high_halves(qh, A3, DH ** -0.5)
                high_halves(kh, B3, 1.0)

                def sample_values(b):
                    do(svT[:, bass.ds(j, 1), :], psum[:, b:b + 1, TP - CHUNKS[2][0]:T - CHUNKS[2][0]], ACT.Copy)\
                        .then_inc(sem("svT_ready"), 1)
                high_halves(vh, B3, 1.0, sample_values)
                row_copy(0)
                skip(K_TURN)
                for g, b in enumerate(V_TURN):
                    filled(b)
                    if g < 2:
                        read(b, do(vx[:, 4 * g:4 * g + 4, :].rearrange("p t (b c) -> p t b c", c=DH)[:, :, 0:3:2, :],
                                   bank(b).rearrange("p (t h c) -> p t h c", t=4, h=2), ACT.Copy))
                    else:
                        do(skv[32:32 + NB, bass.ds(P * j, P)], psum[0:NB, b, P:2 * P], ACT.Copy)\
                            .then_inc(sem("sv_ready"), 1)
                        read(b, do(vx[0:TAIL, 8, :].rearrange("p (b c) -> p b c", c=DH)[:, 0:3:2, :],
                                   psum[0:TAIL, b, 0:P].rearrange("p (h c) -> p h c", h=2), ACT.Copy))
                for b in V_TURN + K_TURN:
                    settled(b)
                act.sem_inc(sem("tok_ready"), 1)

                def outputs_high(k):
                    act.wait_ge(sem("o_read"), GROUPS * j + k + 2)
                    h, s = divmod(k, SEGS)
                    rows, n = slice(DH * h, DH * h + DH), min(SEG, TP - SEG * s)
                    do(oh[rows, bass.ds(j, 1), SEG * s:SEG * s + n], of[rows, k % 2:k % 2 + 1, 0:n], ACT.Copy)\
                        .then_inc(sem("oh_ready"), 1)

                act.wait_ge(sem("nck_ready"), j + 1)
                for x, (k, l, h, t, c0, n, _) in enumerate(TILES):
                    w = width(t)
                    act.wait_ge(sem("tile_full"), NTILE * j + x + 1)
                    if x >= RING_P:
                        act.wait_ge(sem("mixed_in"), NTILE * j + x - RING_P + 1)
                    do(pt[0:w, x % RING_P, 0:n], psum[0:w, ST_BANKS[x % 3], 0:n], ACT.Exp, bias=nck[0:w, t, h:h + 1])\
                        .then_inc(sem("probs_ready"), 1)
                    if x in ROWS_AT:
                        row_copy(ROWS_AT[x])
                    if x in OUT_AT:
                        outputs_high(OUT_AT.index(x))
                outputs_high(GROUPS - 1)
                act.wait_ge(sem("kv_stored"), KV_STORES * 16 * (j + 1))
                B.end(4)
            act.wait_ge(sem("sv_ready"), 4)
            settled(6)
            act.dma_start(OUT["v_sample"][0, :, 0, :, :].rearrange("b h d -> b (h d)"), skv[32:32 + NB, :])\
                .then_inc(sem("skv_stored"), 16)
            act.dma_start(OUT["k_sample"][0, :, 0, :, :].rearrange("b h d -> b (h d)"), skv[0:NB, :])\
                .then_inc(sem("skv_stored"), 16)

            act.wait_ge(sem("o_done"), 1)
            act.wait_ge(sem("kv_stored"), KV_STORES * 16 * 4)
            act.wait_ge(sem("lf_stored"), 48)
            skip([n % 2 for n in range(NB)] + [2, 3])
            fill(act, 0, 1)
            fill(act, 1, 1)
            for m in range(GH):
                for c, (c0, cw) in enumerate(CHUNKS):
                    b = GATE_BANKS[m][c]
                    filled(b)
                    read(b, do(gated[:, m, c0:c0 + cw], psum[:, b, 0:cw], SILU))
                    if (3 * m + c) % 2:
                        fill(act, 2 + (3 * m + c) // 2, 1)
            fill(act, NB, 1)
            fill(act, NB + 1, 1)
            skip([4, 5])
            act.wait_ge(sem("sdiff_ready"), 2)
            do(spr[:, :, :], spr[:, :, :], ACT.Exp).then_inc(sem("sprobs_ready"), 1)
            do(ss[:, :, :, :], ss[:, :, :, :], ACT.Exp).then_inc(sem("sprobs_ready"), 1)
            for n in range(NB + 2, 2 * NB):
                fill(act, n, 1)
            skip([6, 7] + [n % 2 for n in range(NB)])

            act.wait_ge(sem("samples_done"), 1)
            for i in range(2):
                act.wait_ge(sem("wai_ready"), 2 * i + 2)
                for c, b in enumerate(G_LG):
                    c0, cw = CHUNKS[c]
                    filled(b)
                    do(gy[:, c0:c0 + cw], psum[:, b, 0:cw], ACT.Abs, bias=bai[:, 0:1])\
                        .then_inc(sem("gy_abs"), 1)
                    B.use(b)
                act.wait_ge(sem("gy_abs"), 3 * i + 3)
                do(gy[:, :], gy[:, :], ACT.Exp, scale=-1.0).then_inc(sem("gy_ln"), 1)
                act.wait_ge(sem("gy_ln"), 2 * i + 1)
                do(gy[:, :], gy[:, :], ACT.Ln, bias=1.0).then_inc(sem("gy_ln"), 1)
                act.wait_ge(sem("lg_ready"), i + 1)
                do(eg[:, :], gx[:, TP:T], ACT.Exp, scale=1.0 / TAU).then_inc(sem("eg_ready"), 1)
                act.wait_ge(sem("gd_ready"), 2 * i + 2)
                do(gy[:, 0:TP], gx[:, 0:TP], ACT.Exp, scale=-1.0 / TAU).then_inc(sem("decays"), 1)
                act.wait_ge(sem("decays"), 3 * i + 1)
                do(gx[:, 0:TP], gx[:, 0:TP], ACT.Exp, scale=1.0 / TAU).then_inc(sem("decays"), 1)
                act.wait_ge(sem("gl_ready"), i + 1)
                do(gl[:, :, :], gl[:, :, :], ACT.Exp, scale=1.0 / TAU).then_inc(sem("decays"), 1)
                skip(A3 + B3)
                for c, (c0, cw) in enumerate(CHUNKS):
                    filled(A3[c])
                    read(A3[c], do(gvT[:, c0:c0 + cw], psum[:, A3[c], 0:cw], ACT.Copy))
                for g, b in enumerate(G_KTURN):
                    filled(b)
                    if g < 2:
                        ins = do(ke_tok[:, 4 * g:4 * g + 4, :], bank(b).rearrange("p (t c) -> p t c", t=4),
                                 ACT.Copy)
                    else:
                        ins = do(ke_tok[0:TAIL, 8, :], psum[0:TAIL, b, 0:P], ACT.Copy)
                    read(b, ins)

                def values_turned(v):
                    for g, b in enumerate(G_VTURN[v]):
                        filled(b)
                        cols = slice(v * P, (v + 1) * P)
                        if g < 2:
                            ins = do(vb_tok[:, 4 * g:4 * g + 4, cols],
                                     bank(b).rearrange("p (t c) -> p t c", t=4), ACT.Copy)
                        else:
                            do(vs_tok[:, cols], psum[0:NB, b, P:2 * P], ACT.Copy).then_inc(sem("vs_ready"), 1)
                            ins = do(vb_tok[0:TAIL, 8, cols], psum[0:TAIL, b, 0:P], ACT.Copy)
                        read(b, ins)

                v1 = [(b, B.after(b)) for b in B3]
                skip(B3)
                values_turned(0)
                for c, (c0, cw) in enumerate(CHUNKS):
                    b, full = v1[c]
                    act.wait_ge(bank_full[b], full)
                    do(gvT[:, c0:c0 + cw], psum[:, b, 0:cw], ACT.Copy).then_inc(bank_free[b], 1)
                values_turned(1)
                for c in range(NT + 1):
                    if c < NT:
                        skip([2 * (c % 2), 6 + c % 2])
                    if c > 0:
                        q, n = c - 1, width(c - 1)
                        b = 4 + q % 2
                        filled(b)
                        src = psum[:, b, 0:2 * P].rearrange("p (h c) -> p h c", h=2)[:, :, 0:n]
                        do(go[:, :, q * P:q * P + n], src, ACT.Copy).then_inc(sem("go_ready"), 1)
                        read(b, do(gsq[:, :, q * P:q * P + n], src, ACT.Square))
                skip(G_VB)
                filled(G_OS)
                src = psum[:, G_OS:G_OS + 2, 0:NB]
                do(go[:, :, TP:T], src, ACT.Copy).then_inc(sem("go_ready"), 1)
                read(G_OS, do(gsq[:, :, TP:T], src, ACT.Square))
                act.wait_ge(sem("state_ready"), NT * i + NT)
                for hh_ in range(2):
                    rows = slice(64 * hh_, 64 * hh_ + 64)
                    act.dma_start(OUT["gla_prompt"][0, 0, bass.ds(2 * i + hh_, 1), :, :]
                                  .rearrange("h d v -> (h d) v"), stt[rows, :]).then_inc(sem("stt_stored"), 16)
                act.wait_ge(sem("sst_ready"), NB * i + NB)
                for hh_ in range(2):
                    rows = slice(64 * hh_, 64 * hh_ + 64)
                    act.dma_start(OUT["gla_sample"][0][:, bass.ds(2 * i + hh_, 1), :, :]
                                  .rearrange("b h d v -> d (b h) v"), sst[rows, :, :])\
                        .then_inc(sem("sst_stored"), 16)
                for h in range(2):
                    for c, (c0, cw) in enumerate(CHUNKS):
                        b = (A3, B3)[h][c]
                        filled(b)
                        read(b, do(gsq[:, h, c0:c0 + cw], psum[:, b, 0:cw], ACT.Ln, scale=1.0 / GDV,
                                   bias=eps[:, 0:1]))
                for h in range(2):
                    for b in (A3, B3)[h]:
                        settled(b)
                    do(gsq[:, h, :], gsq[:, h, :], ACT.Exp, scale=-0.5).then_inc(sem("root_ready"), 1)
            act.wait_ge(sem("stt_stored"), 64)
            act.wait_ge(sem("sst_stored"), 64)
            act.wait_ge(sem("gated_ready"), 4)
            for h in range(GH):
                do(oh[:, 4 + h, :], gated[:, h, :], ACT.Copy).then_inc(sem("og_high"), 1)

            with act.Fori(0, KT) as m:
                B.loop(m, [2, 2, 2, 2, 2, 2, 0, 0])
                for c, (c0, cw) in enumerate(CHUNKS):
                    filled(A3[c])
                    if c == 0:
                        act.wait_ge(sem("o_split"), 4)
                    read(A3[c], do(mixed[:, bass.ds(m, 1), c0:c0 + cw], psum[:, A3[c]:A3[c] + 1, 0:cw],
                                   ACT.Sigmoid))
                for c, (c0, cw) in enumerate(CHUNKS):
                    filled(B3[c])
                    read(B3[c], do(sgb[:, c0:c0 + cw], psum[:, B3[c], 0:cw], ACT.Sigmoid))
                skip(A3 + B3)
                act.wait_ge(sem("mixed_ready"), 3 * m + 3)
                B.end(KT)
            for c, (c0, cw) in enumerate(CHUNKS):
                for q in range(2):
                    do(oh[:, 4 * q:4 * q + 4, c0:c0 + cw], mixed[:, 4 * q:4 * q + 4, c0:c0 + cw], ACT.Copy)\
                        .then_inc(sem("mixed_high"), 1)
            for m in range(KT):
                skip((A3, B3)[m % 2])

            def norm(tag, eps_col, gain, shift, high):
                skip(MEAN_BANKS)

                def squares(c):
                    c0, cw = CHUNKS[c]
                    act.wait_ge(sem(f"{tag}_dev"), 2 * c + 1)
                    for q in range(2):
                        if q == 1:
                            act.wait_ge(sem(f"{tag}_dev"), 2 * c + 2)
                        do(ysq[:, c % 2, 4 * q:4 * q + 4, 0:cw], mixed[:, 4 * q:4 * q + 4, c0:c0 + cw],
                           ACT.Square).then_inc(sem(f"{tag}_sq"), 1)

                def root(c):
                    c0, cw = CHUNKS[c]
                    b = SQ_BANKS[c]
                    filled(b)
                    ins = do(yrst[:, c0:c0 + cw], psum[:, b, 0:cw], ACT.Sqrt, scale=1.0 / D,
                             bias=eps[:, eps_col:eps_col + 1])
                    read(b, ins)

                def affine(c):
                    c0, cw = CHUNKS[c]
                    for k in range(KT):
                        if k % 4 == 0:
                            act.wait_ge(sem(f"{tag}_norm"), 2 * c + k // 4 + 1)
                        do(mixed[:, k, c0:c0 + cw], mixed[:, k, c0:c0 + cw], ACT.Identity,
                           scale=lnp[:, gain, k:k + 1], bias=lnp[:, shift, k:k + 1]).then_inc(sem(f"{tag}_aff"), 1)
                    if high:
                        for q in range(2):
                            act.wait_ge(sem(f"{tag}_aff"), KT * c + 4 * q + 4)
                            do(xh[:, 4 * q:4 * q + 4, c0:c0 + cw], mixed[:, 4 * q:4 * q + 4, c0:c0 + cw],
                               ACT.Copy).then_inc(sem("x1_high"), 1)
                squares(0)
                squares(1)
                root(0)
                squares(2)
                affine(0)
                root(1)
                affine(1)
                root(2)
                affine(2)
            norm("ln1", 1, 0, 1, True)
            act.wait_ge(sem("x1_split"), 6)
            for k in range(KT):
                do(mixed[:, k, :], mixed[:, k, :], ACT.Copy, scale=ALPHA).then_inc(sem("y_scaled"), 1)

            with act.Fori(0, FGROUPS) as g:
                B.loop(g, FFN_PER)
                for u in range(2):
                    for c, (c0, cw) in enumerate(CHUNKS):
                        filled(A3[c])
                        read(A3[c], do(sg[:, u, c0:c0 + cw], psum[:, A3[c], 0:cw], SILU))
                    skip(B3)
                    for c, (c0, cw) in enumerate(CHUNKS):
                        n = 3 * u + c
                        act.wait_ge(sem("hidden"), 6 * g + n + 1)
                        do(hh[:, u, c0:c0 + cw], hf[:, n % 2, 0:cw], ACT.Copy).then_inc(sem("hidden_high"), 1)
                for c in range(3):
                    skip(OUT_BANKS)
                B.end(FGROUPS)
            norm("ln2", 1, 2, 3, False)

            y_p, y_s = OUT["y_prompt"][0], OUT["y_sample"][:, 0, :]
            for t in range(NT):
                w = P if t < 8 else NB
                b0, b1 = (2 * t) % 6, (2 * t + 1) % 6
                filled(b0)
                if t >= 2:
                    act.wait_ge(sem(f"y_stored{t % 2}"), 16 * (t // 2))
                read(b0, do(yout[0:w, t % 2, 0:512], psum[0:w, b0, :], ACT.Copy))
                B.use(b1)
                settled(b0)
                settled(b1)
                dst = y_p[t * P:(t + 1) * P, :] if t < 8 else y_s
                act.dma_start(dst, yout[0:w, t % 2, :]).then_inc(sem(f"y_stored{t % 2}"), 16)
            act.wait_ge(sem("y_stored0"), 16 * 5)
            act.wait_ge(sem("y_stored1"), 16 * 4)
            act.wait_ge(sem("lf_stored"), 48)
            act.wait_ge(sem("skv_stored"), 32)

        @block.vector
        def _(dve):
            B = Banks()
            ve = nc.vector

            def filled(b):
                dve.wait_ge(bank_full[b], B.after(b))

            def read(b, ins):
                ins.then_inc(bank_free[b], 1)
                B.use(b)

            def settled(b):
                dve.wait_ge(bank_free[b], B.before(b))

            def skip(banks):
                for b in banks:
                    B.use(b)

            chain = [0]

            def link(ins):
                chain[0] += 1
                ins.then_inc(sem("dve_steps"), 1)
                dve.wait_ge(sem("dve_steps"), chain[0])

            for n in range(2 * NT):
                t, g, b = n // 2, n % 2, XT_BANKS[n]
                rows = P if t < 8 else TAIL + NB
                dve.wait_ge(sem("xh_ready"), n + 1)
                src = bank(b).rearrange("p (k c) -> p k c", k=4)[:, :, 0:rows]
                cols = slice(t * P, t * P + rows)
                read(b, ve.tensor_tensor(xl[:, 4 * g:4 * g + 4, cols], src, f(xh[:, 4 * g:4 * g + 4, cols]),
                                         ALU.subtract))
            skip(A3)
            link(ve.memset(lones[:, :], 1.0))
            for b in range(8):
                settled(b)
            link(ve.memset(vx[:, :, DH:2 * DH], 1.0))
            link(ve.memset(nmax[:, :], 0.0))
            dve.wait_ge(sem("fz_ready"), 3)
            link(ve.tensor_scalar(lfT[:, :], fz[:, :], 0.0, None, ALU.min))
            dve.wait_ge(sem("fe"), 3)
            ve.tensor_tensor(lfT[:, :], lfT[:, :], fe[:, :], ALU.subtract).then_inc(sem("lf_ready"), 1)
            dve.wait_ge(sem("lf_ready"), 1)
            ve.tensor_tensor_scan(negc[:, :], lones[:, :], lfT[:, 0:TP], 0.0, ALU.mult, ALU.subtract)\
                .then_inc(sem("negc_ready"), 1)
            filled(3)
            ve.tensor_copy(slf[:, :], psum[0:NB, 3, NT * FH:(NT + 1) * FH]).then_inc(sem("slf_ready"), 1)
            link(ve.tensor_copy(lf_tok[0:TAIL, 8, :], psum[0:TAIL, 3, 8 * FH:9 * FH]))
            read(3, ve.tensor_copy(lf_tok[:, 0:8, :], psum[:, 3, 0:8 * FH].rearrange("p (t h) -> p t h", h=FH)))
            filled(4)
            link(ve.memset(negc_tok[:, 8, :], 0.0))
            link(ve.tensor_copy(negc_tok[0:TAIL, 8, :], psum[0:TAIL, 4, 8 * FH:9 * FH]))
            read(4, ve.tensor_copy(negc_tok[:, 0:8, :], psum[:, 4, 0:8 * FH].rearrange("p (t h) -> p t h", h=FH)))
            settled(4)
            dve.sem_inc(sem("negc_turned"), 1)

            dve.sem_inc(sem("o_read"), 1)
            with dve.Fori(0, 4) as j:
                B.loop(j, PAIR_PER)
                def low_halves(dst, high, banks, n, scale, chunks=(0, 1, 2)):
                    for c in chunks:
                        c0, cw = CHUNKS[c]
                        filled(banks[c])
                        dve.wait_ge(sem("qkv_high"), 9 * j + 3 * n + c + 1)
                        read(banks[c], ve.scalar_tensor_tensor(
                            out=dst[:, c0:c0 + cw], in0=psum[:, banks[c], 0:cw], scalar=scale,
                            in1=f(high[:, c0:c0 + cw]), op0=ALU.mult, op1=ALU.subtract))
                low_halves(ql, qh, A3, 0, DH ** -0.5)
                low_halves(kl, kh, B3, 1, 1.0)
                ve.tensor_copy(nck[:, :, :], negc_tok[:, :, bass.ds(2 * j, 2)]).then_inc(sem("nck_ready"), 1)
                dve.wait_ge(sem("cb_loaded"), 16 * j + 16)
                def maxima(n):
                    h, i = divmod(n, NT)
                    nq, nk = width(i), min(P * (i + 1), TP)
                    dve.wait_ge(sem("scores_full"), NI * j + n + 1)
                    apart(dve)
                    s = psum[0:nq, 0:3, :].rearrange("p b c -> p (b c)")[:, 0:nk]
                    ve.tensor_tensor_reduce(out=s, in0=s, in1=cb[0:nq, h, 0:nk], scale=-1.0, scalar=3e38,
                                            op0=ALU.add, op1=ALU.min, accum_out=nmax[0:nq, n:n + 1])\
                        .then_inc(sem("scores_read"), 1)

                def max_split(k):
                    dve.wait_ge(sem("scores_read"), NI * j + PER_SEG * (k + 1))
                    cols = slice(PER_SEG * k, PER_SEG * (k + 1))
                    ve.tensor_copy(nms[:, cols, 0], nmax[:, cols]).then_inc(sem("max_high"), 1)
                    dve.wait_ge(sem("max_high"), GROUPS * j + k + 1)
                    ve.tensor_tensor(nms[:, cols, 1], nmax[:, cols], f(nms[:, cols, 0]), ALU.subtract)\
                        .then_inc(sem("max_split"), 1)

                def group_maxima(k):
                    for n in range(PER_SEG * k, PER_SEG * k + PER_SEG):
                        maxima(n)
                    max_split(k)

                maxima(0)
                low_halves(vl, vh, B3, 2, 1.0, [0])
                maxima(1)
                maxima(2)
                max_split(0)
                low_halves(vl, vh, B3, 2, 1.0, [1])
                maxima(3)
                maxima(4)
                low_halves(vl, vh, B3, 2, 1.0, [2])
                maxima(5)
                max_split(1)
                for g, b in enumerate(K_TURN):
                    filled(b)
                    if g < 2:
                        ins = ve.tensor_copy(k_tok[:, 4 * g:4 * g + 4, :],
                                             bank(b).rearrange("p (t c) -> p t c", t=4))
                    else:
                        ve.tensor_copy(skv[0:NB, bass.ds(P * j, P)], psum[0:NB, b, P:2 * P])\
                            .then_inc(sem("stok"), 1)
                        ve.tensor_copy(sq_tok[:, bass.ds(P * j, P)], psum[0:NB, b, 2 * P:3 * P])\
                            .then_inc(sem("stok"), 1)
                        ins = ve.tensor_copy(k_tok[0:TAIL, 8, :], psum[0:TAIL, b, 0:P])
                    read(b, ins)
                skip(V_TURN)

                def outputs(k):
                    h, s = divmod(k, SEGS)
                    rows, sums, n = slice(DH * h, DH * h + DH), slice(DH - DH * h, 2 * DH - DH * h), \
                        min(SEG, TP - SEG * s)
                    dve.wait_ge(sem("mixed_in"), NTILE * j + TILES_TO[k])
                    ve.reciprocal(of[rows, k % 2, 0:n], psum[sums, 5 + k % 2, 0:n]).then_inc(sem("recip"), 1)
                    dve.wait_ge(sem("recip"), GROUPS * j + k + 1)
                    ve.tensor_tensor(of[rows, k % 2, 0:n], of[rows, k % 2, 0:n], psum[rows, 5 + k % 2, 0:n],
                                     ALU.mult).then_inc(sem("o_read"), 1)

                def outputs_low(k):
                    dve.wait_ge(sem("oh_ready"), GROUPS * j + k + 1)
                    h, s = divmod(k, SEGS)
                    rows, n = slice(DH * h, DH * h + DH), min(SEG, TP - SEG * s)
                    cols = slice(SEG * s, SEG * s + n)
                    ve.tensor_tensor(ol[rows, bass.ds(j, 1), cols], of[rows, k % 2:k % 2 + 1, 0:n],
                                     f(oh[rows, bass.ds(j, 1), cols]), ALU.subtract).then_inc(sem("ol_ready"), 1)
                group_maxima(2)
                outputs(0)
                group_maxima(3)
                maxima(12)
                outputs_low(0)
                outputs(1)
                maxima(13)
                maxima(14)
                max_split(4)
                maxima(15)
                outputs_low(1)
                outputs(2)
                maxima(16)
                maxima(17)
                max_split(5)
                outputs_low(2)
                for k in range(3, GROUPS):
                    outputs(k)
                    outputs_low(k)
                dve.wait_ge(sem("kv_stored"), KV_STORES * 16 * (j + 1))
                B.end(4)
            dve.wait_ge(sem("ol_ready"), 4 * GROUPS)
            ve.tensor_copy(later_rows[:, :], low[:, :]).then_inc(sem("o_done"), 1)

            dve.wait_ge(sem("stok"), 8)
            link(ve.tensor_tensor(sqk[:, :], sq_tok[:, :], skv[0:NB, :], ALU.mult))
            link(ve.tensor_reduce(sself[:, :], sqk[:, :].rearrange("b (h d) -> b h d", d=DH), AX, ALU.add))

            def diagonal(src, n):
                ve.tensor_tensor(dself[:, :, :], src[:, :].unsqueeze(1).to_broadcast([NB, NB, FH]),
                                 ident[0:NB, 0:NB].unsqueeze(2).to_broadcast([NB, NB, FH]), ALU.mult)\
                    .then_inc(sem("dself_ready"), 1)
                dve.wait_ge(sem("dself_ready"), n)
            diagonal(sself, 1)
            dve.wait_ge(sem("lf_loaded"), 16 * NB * NPAGE)
            link(ve.memset(lfs[:, :, :, :], 0.0))
            for p in reversed(range(NPAGE - 1)):
                link(ve.tensor_tensor(lfs[:, :, p, :], lfs[:, :, p + 1, :], lfp[:, :, p + 1, :], ALU.add))
            ve.sem_inc(sem("lfs_ready"), 1)
            filled(2)
            read(2, ve.tensor_copy(sbc[:, :, :], psum[:, 2, 0:64].rearrange("q (b h) -> q b h", b=NB)))
            settled(2)
            diagonal(slf, 2)
            for n in range(NB):
                b = n % 2
                dve.wait_ge(sem(f"kv_loaded{n % 2}"), 16 * NPAGE * (n // 2 + 1))
                filled(b)
                k = kv[n % 2][:, :, :]
                read(b, ve.tensor_tensor(k, k, bank(b).unsqueeze(1).to_broadcast([P, NPAGE, FW]), ALU.mult))
                settled(b)
                ve.tensor_reduce(ss[:, n, :, :], k.rearrange("q p (h d) -> q p h d", d=DH), AX, ALU.add)\
                    .then_inc(sem("kv_used"), 1)
            for m in range(GH):
                skip(GATE_BANKS[m])
            dve.wait_ge(sem("kv_used"), NB)
            filled(3)
            whole = ss[:, :, :, :].rearrange("q b p h -> q (b p h)")
            read(3, ve.tensor_tensor(whole, whole, bank(3), ALU.add))
            settled(3)
            link(ve.tensor_reduce(mx[:, :, :], ss[:, :, :, :].rearrange("q b p h -> q b h p"), AX, ALU.max))
            ve.tensor_tensor(mx[:, :, :], mx[:, :, :], sbc[:, :, :], ALU.max).then_inc(sem("mx_ready"), 1)
            filled(4)
            read(4, ve.tensor_reduce(mcol[:, :], psum[0:64, 4, 0:P], AX, ALU.max))
            settled(4)
            ve.tensor_scalar(dmx[:, :], ident[0:64, 0:64], mcol[:, 0:1], None, ALU.mult)\
                .then_inc(sem("dmx_ready"), 1)
            filled(5)
            read(5, ve.tensor_copy(mbc[:, :, :], psum[:, 5, 0:64].rearrange("q (b h) -> q b h", b=NB)))
            settled(5)
            ve.tensor_tensor(spr[:, :, :], sbc[:, :, :], mbc[:, :, :], ALU.subtract).then_inc(sem("sdiff_ready"), 1)
            ve.tensor_tensor(ss[:, :, :, :], ss[:, :, :, :],
                             mbc[:, :, :].unsqueeze(2).to_broadcast([P, NB, NPAGE, FH]), ALU.subtract)\
                .then_inc(sem("sdiff_ready"), 1)
            filled(6)
            read(6, ve.tensor_reduce(den[:, :, :], bank(6).rearrange("q (b p h) -> q b h p", b=NB, p=NPAGE),
                                     AX, ALU.add))
            settled(6)
            dve.wait_ge(sem("sprobs_ready"), 2)
            link(ve.tensor_tensor(den[:, :, :], den[:, :, :], spr[:, :, :], ALU.add))
            link(ve.reciprocal(den[:, :, :], den[:, :, :]))
            for n in range(NB):
                b = n % 2
                filled(b)
                if n < NB - 2:
                    dve.sem_inc(sem("kv_used"), 1)
                read(b, ve.tensor_tensor(own_v[b][:, :].rearrange("h (g d) -> h g d", d=DH),
                                         psum[0:FH, b, :].rearrange("h (g d) -> h g d", d=DH),
                                         ident[0:FH, 0:FH].unsqueeze(2).to_broadcast([FH, FH, DH]), ALU.mult))
            dve.wait_ge(sem("svT_ready"), 4)
            filled(7)
            for hh_ in range(2):
                rows = slice(64 * hh_, 64 * hh_ + 64)
                own = spr[rows, :, :].rearrange("q b (m e) -> q e m b", e=2)[:, hh_, :, :]
                dd = den[rows, :, :].rearrange("q b (m e) -> q e m b", e=2)[:, hh_, :, :]
                po = psum[rows, 7, 0:4 * NB].rearrange("q (m b) -> q m b", m=4)
                o = onum[rows, :, :]
                link(ve.tensor_tensor(o, own, svT[rows, :, :], ALU.mult))
                if hh_ == 0:
                    link(ve.tensor_tensor(o, po, o, ALU.add))
                else:
                    read(7, ve.tensor_tensor(o, po, o, ALU.add))
                    settled(7)
                link(ve.tensor_tensor(o, o, dd, ALU.mult))
            link(ve.tensor_copy(oh[:, 0:4, TP:T], onum[:, :, :]))
            ve.tensor_tensor(ol[:, 0:4, TP:T], onum[:, :, :], f(oh[:, 0:4, TP:T]), ALU.subtract)\
                .then_inc(sem("samples_done"), 1)
            dve.wait_ge(sem("samples_done"), 1)
            dve.wait_ge(sem("skv_stored"), 32)

            steps = [0]

            def step(ins):
                steps[0] += 1
                ins.then_inc(sem("gla_steps"), 1)
                dve.wait_ge(sem("gla_steps"), steps[0])
            link(ve.memset(stp[:, :, :, :], 0.0))
            for i in range(2):
                ve.tensor_copy(wai[:, :], wa2[:, bass.ds(P * i, P)]).then_inc(sem("wai_ready"), 1)
                ve.tensor_copy(bai[:, :], bac[:, bass.ds(i, 1)]).then_inc(sem("wai_ready"), 1)
                dve.wait_ge(sem("wai_ready"), 2 * i + 2)
                for c, b in enumerate(G_LG):
                    c0, cw = CHUNKS[c]
                    filled(b)
                    dve.wait_ge(sem("gy_abs"), 3 * i + c + 1)
                    read(b, ve.tensor_scalar(gx[:, c0:c0 + cw], psum[:, b, 0:cw], bai[:, 0:1], 0.0,
                                             ALU.add, ALU.min))
                settled(6)
                settled(7)
                dve.wait_ge(sem("gy_ln"), 2 * i + 2)
                ve.tensor_tensor(gx[:, :], gx[:, :], gy[:, :], ALU.subtract).then_inc(sem("lg_ready"), 1)
                dve.wait_ge(sem("lg_ready"), i + 1)
                for c in range(NT):
                    cols = slice(c * P, c * P + width(c))
                    step(ve.tensor_tensor_scan(gy[:, cols], ones[:, 0:width(c)], gx[:, cols], 0.0,
                                               ALU.mult, ALU.add))
                full = gy[:, 0:8 * P].rearrange("p (c t) -> p c t", t=P)
                step(ve.tensor_copy(gl[:, 0, 0:8], full[:, :, P - 1]))
                step(ve.tensor_copy(gl[:, 0, 8:9], gy[:, TP - 1:TP]))
                step(ve.tensor_copy(gl[:, 2, 0:8], full[:, :, P // 2 - 1]))
                step(ve.tensor_copy(gl[:, 2, 8:9], gy[:, 8 * P + TAIL // 2 - 1:8 * P + TAIL // 2]))
                dve.wait_ge(sem("eg_ready"), i + 1)
                ve.tensor_tensor(gx[:, 0:8 * P].rearrange("p (c t) -> p c t", t=P), full,
                                 gl[:, 2, 0:8].unsqueeze(2).to_broadcast([P, 8, P]), ALU.subtract)\
                    .then_inc(sem("gd_ready"), 1)
                ve.tensor_scalar(gx[:, 8 * P:TP], gy[:, 8 * P:TP], gl[:, 2, 8:9], None, ALU.subtract)\
                    .then_inc(sem("gd_ready"), 1)
                ve.tensor_tensor(gl[:, 1, :], gl[:, 0, :], gl[:, 2, :], ALU.subtract).then_inc(sem("gl_ready"), 1)
                step(ve.memset(gx[:, TP:T], 1.0))
                step(ve.memset(gy[:, TP:T], 1.0))
                dve.wait_ge(sem("decays"), 3 * i + 3)
                for c, (c0, cw) in enumerate(CHUNKS):
                    filled(A3[c])
                    read(A3[c], ve.scalar_tensor_tensor(out=qe[:, c0:c0 + cw], in0=psum[:, A3[c], 0:cw],
                                                        scalar=GDK ** -0.5, in1=gx[:, c0:c0 + cw],
                                                        op0=ALU.mult, op1=ALU.mult))
                for c, (c0, cw) in enumerate(CHUNKS):
                    filled(B3[c])
                    read(B3[c], ve.tensor_tensor(ke[:, c0:c0 + cw], psum[:, B3[c], 0:cw], gy[:, c0:c0 + cw],
                                                 ALU.mult))
                skip(A3 + G_KTURN + B3 + G_VTURN[0] + G_VTURN[1])
                dve.wait_ge(sem("sst_loaded"), 32 * i + 32)
                ve.tensor_tensor(sst[:, :, :], sst[:, :, :], eg[:, :].unsqueeze(2).to_broadcast([P, NB, P]),
                                 ALU.mult).then_inc(sem("sst_faded"), 1)
                dve.wait_ge(sem("sst_faded"), i + 1)
                for m in range(4):
                    b = G_VB[m]
                    filled(b)
                    for q in range(2):
                        n = 2 * m + q
                        for h in range(2):
                            rows = slice(64 * h, 64 * h + 64)
                            ins = ve.scalar_tensor_tensor(
                                out=sst[rows, n, :], in0=psum[rows, b, 256 * q + P * h:256 * q + P * h + P],
                                scalar=ke[rows, TP + n:TP + n + 1], in1=sst[rows, n, :], op0=ALU.mult,
                                op1=ALU.add)
                            if q == 1 and h == 1:
                                read(b, ins)
                            else:
                                ins.then_inc(sem("sst_part"), 1)
                for b in (6, 7):
                    settled(b)
                dve.wait_ge(sem("sst_part"), 12 * (i + 1))
                ve.sem_inc(sem("sst_ready"), NB)
                for c in range(NT):
                    n, par, b = width(c), c % 2, 2 * (c % 2)
                    filled(b)
                    if c >= 2:
                        dve.wait_ge(bank_full[4 + par], B.before(4 + par))
                    read(b, ve.tensor_tensor(gsc[0:n, par, :, 0:n],
                                             psum[0:n, b:b + 2, 0:n],
                                             tri[0:n, 0:n].unsqueeze(1).to_broadcast([n, 2, n]), ALU.mult))
                    filled(6 + par)
                    for h in range(2):
                        rows = slice(64 * h, 64 * h + 64)
                        ins = ve.tensor_scalar(kvs[rows, :], psum[rows, 6 + par, h * P:(h + 1) * P],
                                               gl[rows, 1, c:c + 1], None, ALU.mult)
                        if h == 1:
                            read(6 + par, ins)
                        else:
                            ins.then_inc(sem("kvs_half"), 1)
                    settled(6 + par)
                    dve.wait_ge(sem("kvs_half"), NT * i + c + 1)
                    if c == 0:
                        ins = ve.tensor_copy(stt[:, :], kvs[:, :])
                    else:
                        ins = ve.scalar_tensor_tensor(out=stt[:, :], in0=stt[:, :], scalar=gl[:, 0, c:c + 1],
                                                      in1=kvs[:, :], op0=ALU.mult, op1=ALU.add)
                    ins.then_inc(sem("state_ready"), 1)
                    dve.wait_ge(sem("state_ready"), NT * i + c + 1)
                    if c > 0:
                        skip([4 + (c - 1) % 2])
                    if c < NT - 1:
                        if c > 0:
                            dve.wait_ge(bank_full[4 + (c - 1) % 2], B.before(4 + (c - 1) % 2))
                        for h in range(2):
                            rows = slice(64 * h, 64 * h + 64)
                            ins = ve.tensor_scalar(stp[rows, (c + 1) % 2, h, :], stt[rows, :],
                                                   gl[rows, 2, c + 1:c + 2], None, ALU.mult)
                            if h == 1:
                                ins.then_inc(sem("stp_ready"), 1)
                            else:
                                ins.then_inc(sem("stp_half"), 1)
                skip([4 + (NT - 1) % 2])
                skip([G_OS] + A3 + B3)
                dve.wait_ge(sem("go_ready"), 10 * i + 10)
                for h in range(2):
                    dve.wait_ge(sem("root_ready"), 2 * i + h + 1)
                    step(ve.tensor_tensor(go[:, h, :], go[:, h, :], gsq[:, h, :], ALU.mult))
                    g1 = gated[:, bass.ds(2 * i + h, 1), :]
                    ve.scalar_tensor_tensor(out=g1, in0=go[:, h:h + 1, :], scalar=gng[:, 0:1], in1=g1,
                                            op0=ALU.mult, op1=ALU.mult).then_inc(sem("gated_ready"), 1)
                dve.wait_ge(sem("gated_ready"), 2 * i + 2)
                dve.wait_ge(sem("stt_stored"), 32 * i + 32)
                dve.wait_ge(sem("sst_stored"), 32 * i + 32)
            for h in range(GH):
                dve.wait_ge(sem("og_high"), h + 1)
                ve.tensor_tensor(ol[:, 4 + h, :], gated[:, h, :], f(oh[:, 4 + h, :]), ALU.subtract)\
                    .then_inc(sem("o_split"), 1)

            with dve.Fori(0, KT) as m:
                B.loop(m, [2, 2, 2, 2, 2, 2, 0, 0])
                skip(A3 + B3)
                for c, (c0, cw) in enumerate(CHUNKS):
                    b = A3[c]
                    filled(b)
                    mx_ = mixed[:, bass.ds(m, 1), c0:c0 + cw]
                    read(b, ve.tensor_tensor(mx_, mx_, psum[:, b:b + 1, 0:cw], ALU.mult))
                for c, (c0, cw) in enumerate(CHUNKS):
                    b = B3[c]
                    filled(b)
                    s_ = sgb[:, c0:c0 + cw]
                    read(b, ve.tensor_tensor(s_, s_, psum[:, b, 0:cw], ALU.mult))
                    settled(A3[c])
                    settled(b)
                    mx_ = mixed[:, bass.ds(m, 1), c0:c0 + cw]
                    ve.tensor_tensor(mx_, mx_, sgb[:, c0:c0 + cw].unsqueeze(1), ALU.add)\
                        .then_inc(sem("mixed_ready"), 1)
                B.end(KT)
            for c, (c0, cw) in enumerate(CHUNKS):
                for q in range(2):
                    dve.wait_ge(sem("mixed_high"), 2 * c + q + 1)
                    four = slice(4 * q, 4 * q + 4)
                    ve.tensor_tensor(ol[:, four, c0:c0 + cw], mixed[:, four, c0:c0 + cw],
                                     f(oh[:, four, c0:c0 + cw]), ALU.subtract).then_inc(sem("mixed_split"), 1)
            dve.wait_ge(sem("mixed_split"), 6)
            n = 0
            for m in range(KT):
                for c, (c0, cw) in enumerate(CHUNKS):
                    b = (A3, B3)[m % 2][c]
                    cols = slice(c0, c0 + cw)
                    y = mixed[:, m, cols]
                    filled(b)
                    read(b, ve.scalar_tensor_tensor(out=y, in0=f(xh[:, m, cols]), scalar=ALPHA,
                                                    in1=psum[:, b, 0:cw], op0=ALU.mult, op1=ALU.add))
                    settled(b)
                    ve.scalar_tensor_tensor(out=y, in0=f(xl[:, m, cols]), scalar=ALPHA, in1=y,
                                            op0=ALU.mult, op1=ALU.add).then_inc(sem("residual"), 1)
                    n += 1
                    dve.wait_ge(sem("residual"), n)
                    if m == 0:
                        ins = ve.tensor_copy(ysum[:, cols], y)
                    else:
                        dve.wait_ge(sem("ysum_part"), n - 3)
                        ins = ve.tensor_tensor(ysum[:, cols], ysum[:, cols], y, ALU.add)
                    ins.then_inc(sem("ln1_sum") if m == KT - 1 else sem("ysum_part"), 1)

            def norm(tag, low_too, tile_sums=None):
                mean_full = []
                for b in MEAN_BANKS:
                    mean_full.append(B.after(b))
                    B.use(b)
                sq_free = []
                for b in SQ_BANKS:
                    B.use(b)
                    sq_free.append(B.before(b))

                def deviations(c):
                    c0, cw = CHUNKS[c]
                    b = MEAN_BANKS[c]
                    dve.wait_ge(bank_full[b], mean_full[c])
                    for q in range(2):
                        y = mixed[:, 4 * q:4 * q + 4, c0:c0 + cw]
                        ve.scalar_tensor_tensor(out=y, in0=psum[:, b, 0:cw].unsqueeze(1).to_broadcast([P, 4, cw]),
                                                scalar=-1.0 / D, in1=y, op0=ALU.mult, op1=ALU.add)\
                            .then_inc(sem(f"{tag}_dev"), 1)
                    dve.wait_ge(sem(f"{tag}_dev"), 2 * c + 2)
                    dve.sem_inc(bank_free[b], 1)

                def normalise(c):
                    c0, cw = CHUNKS[c]
                    dve.wait_ge(bank_free[SQ_BANKS[c]], sq_free[c])
                    r = yrst[:, c0:c0 + cw]
                    ve.reciprocal(r, r).then_inc(sem(f"{tag}_root"), 1)
                    dve.wait_ge(sem(f"{tag}_root"), c + 1)
                    for q in range(2):
                        y = mixed[:, 4 * q:4 * q + 4, c0:c0 + cw]
                        ve.tensor_tensor(y, y, r.unsqueeze(1).to_broadcast([P, 4, cw]), ALU.mult)\
                            .then_inc(sem(f"{tag}_norm"), 1)

                def lows(c):
                    if not low_too:
                        return
                    c0, cw = CHUNKS[c]
                    for q in range(2):
                        four = slice(4 * q, 4 * q + 4)
                        dve.wait_ge(sem("x1_high"), 2 * c + q + 1)
                        ve.tensor_tensor(xl[:, four, c0:c0 + cw], mixed[:, four, c0:c0 + cw],
                                         f(xh[:, four, c0:c0 + cw]), ALU.subtract).then_inc(sem("x1_split"), 1)
                if tile_sums is not None:
                    tile_sums(0)
                    tile_sums(1)
                deviations(0)
                if tile_sums is not None:
                    tile_sums(2)
                deviations(1)
                deviations(2)
                normalise(0)
                normalise(1)
                lows(0)
                normalise(2)
                lows(1)
                lows(2)
            norm("ln1", True)
            dve.wait_ge(sem("y_scaled"), KT)

            with dve.Fori(0, FGROUPS) as g:
                B.loop(g, FFN_PER)
                for u in range(2):
                    skip(A3)
                    for c, (c0, cw) in enumerate(CHUNKS):
                        n, b = 3 * u + c, B3[c]
                        settled(A3[c])
                        filled(b)
                        ve.tensor_tensor(hf[:, n % 2, 0:cw], sg[:, u, c0:c0 + cw], psum[:, b, 0:cw], ALU.mult)\
                            .then_inc(sem("hidden"), 1)
                        B.use(b)
                        dve.wait_ge(sem("hidden_high"), 6 * g + n + 1)
                        ve.tensor_tensor(hl[:, u, c0:c0 + cw], hf[:, n % 2, 0:cw], f(hh[:, u, c0:c0 + cw]),
                                         ALU.subtract).then_inc(sem("hidden_split"), 1)
                        dve.sem_inc(bank_free[b], 1)
                for c, (c0, cw) in enumerate(CHUNKS):
                    for m in range(KT):
                        b = OUT_BANKS[m]
                        filled(b)
                        y = mixed[:, m, c0:c0 + cw]
                        read(b, ve.tensor_tensor(y, y, psum[:, b, 0:cw], ALU.add))
                for b in range(8):
                    settled(b)
                B.end(FGROUPS)

            def tile_sums(c):
                c0, cw = CHUNKS[c]
                ve.tensor_reduce(ysum[:, c0:c0 + cw], mixed[:, :, c0:c0 + cw].rearrange("p k t -> p t k"), AX,
                                 ALU.add).then_inc(sem("ln2_sum"), 1)
            norm("ln2", False, tile_sums)
            for t in range(NT):
                w = P if t < 8 else NB
                b0, b1 = (2 * t) % 6, (2 * t + 1) % 6
                B.use(b0)
                filled(b1)
                if t >= 2:
                    dve.wait_ge(sem(f"y_stored{t % 2}"), 16 * (t // 2))
                read(b1, ve.tensor_copy(yout[0:w, t % 2, 512:1024], psum[0:w, b1, :]))


_OUTS = [("y_prompt", (1, SEQ, D)), ("y_sample", (NB, 1, D)),
         ("k_prompt", (1, 1, TP, FH, DH)), ("v_prompt", (1, 1, TP, FH, DH)), ("lf_prompt", (1, 1, TP, FH)),
         ("gla_prompt", (1, 1, GH, GDK, GDV)),
         ("k_sample", (1, NB, 1, FH, DH)), ("v_sample", (1, NB, 1, FH, DH)), ("lf_sample", (1, NB, 1, FH)),
         ("gla_sample", (1, NB, GH, GDK, GDV))]


def kernel(**inputs):
    import numpy as _np
    import concourse.bacc as _bacc
    from concourse.bass_utils import run_bass_kernel_spmd as _run

    nc = _bacc.Bacc("TRN2", target_bir_lowering=False, num_devices=1)
    arrays, ins, outs = {}, {}, {}
    for name in inputs:
        a = _np.ascontiguousarray(inputs[name])
        arrays[f"in_{name}"] = a
        ins[name] = nc.dram_tensor(f"in_{name}", a.shape, mybir.dt.from_np(a.dtype), kind="ExternalInput").ap()
    for name, shape in _OUTS:
        outs[name] = nc.dram_tensor(f"out_{name}", shape, F32, kind="ExternalOutput").ap()
    build(nc, ins, outs)
    r = _run(nc, [arrays], core_ids=[0])
    return tuple(r.results[0][f"out_{name}"] for name, _ in _OUTS)
```
